# Optimizing a Trainium2 kernel written in Bass

```python
import jax, jax.numpy as jnp
from jax import lax
import numpy as np

D_MODEL = 1024
BATCH = 1
SEQ = 128
DEPTH = 1
DEC_BATCH = 1
DEC_SEQ = 512
PAST_LEN = 128

GRID_W = 64
MIX_W = D_MODEL
LRU_W = MIX_W // 2
LRU_BLOCKS = 8
LRU_BS = LRU_W // LRU_BLOCKS
LRU_CONV = 4
LRU_PAD_L = 2
LRU_PAD_R = 1
RGLRU_C = 8.0
GLA_W = MIX_W - LRU_W
GLA_HEADS = 4
GLA_DV = GLA_W // GLA_HEADS
GLA_DK = GLA_DV // 2
GLA_QK = GLA_HEADS * GLA_DK
GLA_RANK = 16
GLA_TAU = 16.0
GLA_CHUNK = 64
N_GROUPS = 4
EXP_PER_GROUP = 4
N_EXPERTS = N_GROUPS * EXP_PER_GROUP
TOP_K_IN_GROUP = 2
D_EXPERT = 256
EPS = 1e-6
IN_SIZES = (LRU_W, LRU_W, GLA_QK, GLA_QK, GLA_W, GLA_W, 2 * GLA_RANK)
IN_SPLITS = tuple(int(s) for s in np.cumsum(IN_SIZES)[:-1])
IN_COLS = int(sum(IN_SIZES))

kernel_name = "hybrid_lru_gla_hmoe_diffusion_step"

def rmsnorm(x, g):
    x32 = x.astype(jnp.float32)
    y = x32 * lax.rsqrt(jnp.mean(x32 * x32, axis=-1, keepdims=True) + EPS)
    return (y * g.astype(jnp.float32)).astype(x.dtype)

def centred_conv(x, w, b):
    L = x.shape[-2]
    pad = [(0, 0)] * (x.ndim - 2) + [(LRU_PAD_L, LRU_PAD_R), (0, 0)]
    xp = jnp.pad(x, pad)
    y = b.astype(x.dtype)
    for j in range(LRU_CONV):
        y = y + xp[..., j:j + L, :] * w[j].astype(x.dtype)
    return y

def rglru_scan(x, logit_r, logit_i, lam, h0, reverse):
    log_a = RGLRU_C * jax.nn.sigmoid(logit_r) * jax.nn.log_sigmoid(lam.astype(jnp.float32))
    a = jnp.exp(log_a)
    bterm = jnp.sqrt(-jnp.expm1(2.0 * log_a)) * jax.nn.sigmoid(logit_i) * x
    idx = -1 if reverse else 0
    bterm = bterm.at[:, idx].add(a[:, idx] * h0)

    def comb(e1, e2):
        a1, b1 = e1
        a2, b2 = e2
        return a1 * a2, a2 * b1 + b2

    _, h = lax.associative_scan(comb, (a, bterm), reverse=reverse, axis=1)
    h_fin = h[:, 0] if reverse else h[:, -1]
    return h, h_fin

def gla_scan(q, k, v, logg, s0):
    B, H, T, _ = q.shape
    N = T // GLA_CHUNK
    rs = lambda t: t.reshape(B, H, N, GLA_CHUNK, t.shape[-1])
    q, k, v, logg = rs(q), rs(k), rs(v), rs(logg)
    b = jnp.cumsum(logg, axis=3)
    b_ref = b[:, :, :, GLA_CHUNK // 2 - 1:GLA_CHUNK // 2, :]
    b_last = b[:, :, :, -1:, :]
    att = jnp.einsum('bhnid,bhnjd->bhnij', q * jnp.exp(b - b_ref), k * jnp.exp(b_ref - b))
    mask = jnp.tril(jnp.ones((GLA_CHUNK, GLA_CHUNK), dtype=bool))
    att = jnp.where(mask, att, 0.0)
    o_intra = jnp.einsum('bhnij,bhnjv->bhniv', att, v)
    q_in = q * jnp.exp(b)
    kv = jnp.einsum('bhnjd,bhnjv->bhndv', k * jnp.exp(b_last - b), v)
    decay = jnp.exp(b_last[:, :, :, 0, :])

    def step(s, inp):
        q_c, kv_c, d_c = inp
        o = jnp.einsum('bhid,bhdv->bhiv', q_c, s)
        return d_c[..., None] * s + kv_c, o

    s_fin, o_inter = lax.scan(step, s0, (jnp.moveaxis(q_in, 2, 0), jnp.moveaxis(kv, 2, 0),
                                         jnp.moveaxis(decay, 2, 0)))
    o = o_intra + jnp.moveaxis(o_inter, 0, 2)
    return o.reshape(B, H, T, v.shape[-1]), s_fin

def mixer(h, on_grid, s_lru, s_gla, w_in, conv_w, conv_b, lru_wr, lru_br, lru_wi, lru_bi, lru_lam,
          gla_wg, gla_bg, gla_norm_g, w_out):
    B, T, _ = h.shape
    dt = h.dtype
    f32 = jnp.float32
    z = jnp.einsum('btd,de->bte', h, w_in)
    xl, yl, q, k, v, og, gdn = jnp.split(z, IN_SPLITS, axis=-1)

    if on_grid:
        rows = T // GRID_W
        xc = centred_conv(xl.reshape(B, rows, GRID_W, LRU_W), conv_w, conv_b).reshape(B, T, LRU_W)
    else:
        xc = centred_conv(xl, conv_w, conv_b)
    xc = xc.astype(f32)
    xb = xc.reshape(B, T, LRU_BLOCKS, LRU_BS)
    lr = jnp.einsum('btnc,sncd->sbtnd', xb, lru_wr.astype(f32)).reshape(2, B, T, LRU_W) \
        + lru_br.astype(f32)[:, None, None, :]
    li = jnp.einsum('btnc,sncd->sbtnd', xb, lru_wi.astype(f32)).reshape(2, B, T, LRU_W) \
        + lru_bi.astype(f32)[:, None, None, :]
    s_lru = s_lru.astype(f32)
    h_f, sf_f = rglru_scan(xc, lr[0], li[0], lru_lam[0], s_lru[:, 0], False)
    h_b, sf_b = rglru_scan(xc, lr[1], li[1], lru_lam[1], s_lru[:, 1], True)
    lru_out = jax.nn.gelu(yl) * (h_f + h_b).astype(dt)
    new_lru = jnp.stack([sf_f, sf_b], axis=1)

    heads = lambda t, d: t.reshape(B, T, GLA_HEADS, d).transpose(0, 2, 1, 3).astype(f32)
    qh = heads(q, GLA_DK) * (GLA_DK ** -0.5)
    kh = heads(k, GLA_DK)
    vh = heads(v, GLA_DV)
    glog = jnp.einsum('btsr,srk->sbtk', gdn.reshape(B, T, 2, GLA_RANK).astype(f32), gla_wg.astype(f32)) \
        + gla_bg.astype(f32)[:, None, None, :]
    glog = jax.nn.log_sigmoid(glog) / GLA_TAU
    g_f = heads(glog[0], GLA_DK)
    g_b = heads(glog[1], GLA_DK)
    s_gla = s_gla.astype(f32)
    o_f, S_f = gla_scan(qh, kh, vh, g_f, s_gla[:, 0])
    fl = lambda t: jnp.flip(t, axis=2)
    o_b, S_b = gla_scan(fl(qh), fl(kh), fl(vh), fl(g_b), s_gla[:, 1])
    o = o_f + fl(o_b)
    o = o * lax.rsqrt(jnp.mean(o * o, axis=-1, keepdims=True) + EPS) * gla_norm_g.astype(f32)
    o = o.transpose(0, 2, 1, 3).reshape(B, T, GLA_W).astype(dt) * jax.nn.silu(og)
    new_gla = jnp.stack([S_f, S_b], axis=1)

    out = jnp.einsum('bte,ed->btd', jnp.concatenate([lru_out, o], axis=-1), w_out)
    return out, new_lru, new_gla

def hier_moe(h, router_gw, router_gb, router_ew, router_eb, exp_w13, exp_w2):
    B, T, D = h.shape
    dt = h.dtype
    xt = h.reshape(B * T, D)
    lg = (xt @ router_gw + router_gb).astype(jnp.float32)
    pg = jax.nn.softmax(lg, axis=-1)
    gsel = jnp.argmax(lg, axis=-1)
    pg_sel = jnp.take_along_axis(pg, gsel[:, None], axis=1)[:, 0]
    le = (xt @ router_ew + router_eb).astype(jnp.float32).reshape(B * T, N_GROUPS, EXP_PER_GROUP)
    le_sel = jnp.take_along_axis(le, gsel[:, None, None], axis=1)[:, 0]
    pe = jax.nn.softmax(le_sel, axis=-1)
    topv, topi = lax.top_k(pe, TOP_K_IN_GROUP)
    topv = topv / jnp.sum(topv, axis=-1, keepdims=True)
    w_grp = jnp.sum(jax.nn.one_hot(topi, EXP_PER_GROUP, dtype=jnp.float32) * topv[..., None], axis=1)
    gate = (jax.nn.one_hot(gsel, N_GROUPS, dtype=jnp.float32)[:, :, None]
            * (pg_sel[:, None] * w_grp)[:, None, :]).reshape(B * T, N_EXPERTS).astype(dt)
    hid = jnp.einsum('nd,edf->nef', xt, exp_w13)
    a, bgl = jnp.split(hid, 2, axis=-1)
    act = jax.nn.silu(a) * bgl * gate[:, :, None]
    out = jnp.einsum('nef,efd->nd', act, exp_w2)
    return out.reshape(B, T, D)

def block(x, mod, on_grid, s_lru, s_gla, norm1_g, w_in, conv_w, conv_b, lru_wr, lru_br, lru_wi, lru_bi,
          lru_lam, gla_wg, gla_bg, gla_norm_g, w_out, norm2_g, router_gw, router_gb, router_ew, router_eb,
          exp_w13, exp_w2):
    shift1, scale1, gate1, shift2, scale2, gate2 = jnp.split(mod.astype(x.dtype), 6, axis=-1)
    h = rmsnorm(x, norm1_g) * (1.0 + scale1) + shift1
    mix, new_lru, new_gla = mixer(h, on_grid, s_lru, s_gla, w_in, conv_w, conv_b, lru_wr, lru_br, lru_wi,
                                  lru_bi, lru_lam, gla_wg, gla_bg, gla_norm_g, w_out)
    x = x + gate1 * mix
    h = rmsnorm(x, norm2_g) * (1.0 + scale2) + shift2
    x = x + gate2 * hier_moe(h, router_gw, router_gb, router_ew, router_eb, exp_w13, exp_w2)
    return x, new_lru, new_gla

def setup_inputs(seed: int = 0) -> dict:
    key = jax.random.key(seed)
    ks = jax.random.split(key, 32)
    nrm = lambda k, shape, s: jax.random.normal(k, shape, jnp.float32) * s
    a0 = jax.random.uniform(ks[16], (DEPTH, 2, LRU_W), jnp.float32, 0.9, 0.999)
    s = a0 ** (1.0 / RGLRU_C)
    lam = jnp.log(s) - jnp.log1p(-s)
    return {
        "x_prompt": nrm(ks[0], (BATCH, SEQ, D_MODEL), 1.0),
        "x_sample": nrm(ks[1], (DEC_BATCH, DEC_SEQ, D_MODEL), 1.0),
        "state_lru": nrm(ks[2], (DEC_BATCH, DEPTH, 2, LRU_W), 0.5),
        "state_gla": nrm(ks[3], (DEC_BATCH, DEPTH, 2, GLA_HEADS, GLA_DK, GLA_DV), 0.3),
        "c": nrm(ks[4], (DEC_BATCH, D_MODEL), 1.0),
        "c_ctx": nrm(ks[5], (D_MODEL,), 1.0),
        "ada_w": nrm(ks[6], (DEPTH, D_MODEL, 6 * D_MODEL), 0.5 * D_MODEL ** -0.5),
        "ada_b": nrm(ks[7], (DEPTH, 6 * D_MODEL), 0.02),
        "norm1_g": 1.0 + nrm(ks[8], (DEPTH, D_MODEL), 0.02),
        "w_in": nrm(ks[9], (DEPTH, D_MODEL, IN_COLS), D_MODEL ** -0.5),
        "conv_w": nrm(ks[10], (DEPTH, LRU_CONV, LRU_W), LRU_CONV ** -0.5),
        "conv_b": nrm(ks[11], (DEPTH, LRU_W), 0.02),
        "lru_wr": nrm(ks[12], (DEPTH, 2, LRU_BLOCKS, LRU_BS, LRU_BS), LRU_BS ** -0.5),
        "lru_br": nrm(ks[13], (DEPTH, 2, LRU_W), 0.02),
        "lru_wi": nrm(ks[14], (DEPTH, 2, LRU_BLOCKS, LRU_BS, LRU_BS), LRU_BS ** -0.5),
        "lru_bi": nrm(ks[15], (DEPTH, 2, LRU_W), 0.02),
        "lru_lam": lam,
        "gla_wg": nrm(ks[17], (DEPTH, 2, GLA_RANK, GLA_QK), GLA_RANK ** -0.5),
        "gla_bg": nrm(ks[18], (DEPTH, 2, GLA_QK), 0.02),
        "gla_norm_g": 1.0 + nrm(ks[19], (DEPTH, GLA_DV), 0.02),
        "w_out": nrm(ks[20], (DEPTH, MIX_W, D_MODEL), MIX_W ** -0.5),
        "norm2_g": 1.0 + nrm(ks[21], (DEPTH, D_MODEL), 0.02),
        "router_gw": nrm(ks[22], (DEPTH, D_MODEL, N_GROUPS), D_MODEL ** -0.5),
        "router_gb": nrm(ks[23], (DEPTH, N_GROUPS), 0.01),
        "router_ew": nrm(ks[24], (DEPTH, D_MODEL, N_EXPERTS), D_MODEL ** -0.5),
        "router_eb": nrm(ks[25], (DEPTH, N_EXPERTS), 0.01),
        "exp_w13": nrm(ks[26], (DEPTH, N_EXPERTS, D_MODEL, 2 * D_EXPERT), D_MODEL ** -0.5),
        "exp_w2": nrm(ks[27], (DEPTH, N_EXPERTS, D_EXPERT, D_MODEL), D_EXPERT ** -0.5),
        "final_g": 1.0 + nrm(ks[28], (D_MODEL,), 0.02),
    }

def reference(x_prompt, x_sample, state_lru, state_gla, c, c_ctx, ada_w, ada_b, norm1_g, w_in, conv_w,
              conv_b, lru_wr, lru_br, lru_wi, lru_bi, lru_lam, gla_wg, gla_bg, gla_norm_g, w_out, norm2_g,
              router_gw, router_gb, router_ew, router_eb, exp_w13, exp_w2, final_g):
    yp = x_prompt
    ys = x_sample
    Bp = x_prompt.shape[0]
    new_lru = []
    new_gla = []
    for l in range(DEPTH):
        lp = dict(norm1_g=norm1_g[l], w_in=w_in[l], conv_w=conv_w[l], conv_b=conv_b[l], lru_wr=lru_wr[l],
                  lru_br=lru_br[l], lru_wi=lru_wi[l], lru_bi=lru_bi[l], lru_lam=lru_lam[l], gla_wg=gla_wg[l],
                  gla_bg=gla_bg[l], gla_norm_g=gla_norm_g[l], w_out=w_out[l], norm2_g=norm2_g[l],
                  router_gw=router_gw[l], router_gb=router_gb[l], router_ew=router_ew[l],
                  router_eb=router_eb[l], exp_w13=exp_w13[l], exp_w2=exp_w2[l])
        mod_ctx = (jax.nn.silu(c_ctx) @ ada_w[l] + ada_b[l])[None, None, :]
        mod_lat = (jax.nn.silu(c) @ ada_w[l] + ada_b[l])[:, None, :]
        z_lru = jnp.zeros((Bp, 2, LRU_W), jnp.float32)
        z_gla = jnp.zeros((Bp, 2, GLA_HEADS, GLA_DK, GLA_DV), jnp.float32)
        yp, s_l, s_g = block(yp, mod_ctx, False, z_lru, z_gla, **lp)
        new_lru.append(s_l)
        new_gla.append(s_g)
        ys, _, _ = block(ys, mod_lat, True, state_lru[:, l], state_gla[:, l], **lp)
    y_prompt = rmsnorm(yp, final_g)
    y_sample = rmsnorm(ys, final_g)
    state_lru_new = jnp.stack(new_lru, axis=1)
    state_gla_new = jnp.stack(new_gla, axis=1)
    return (y_prompt, y_sample, state_lru_new, state_gla_new)


_drawn_inputs = setup_inputs


def setup_inputs(seed=0):
    import zlib

    import numpy as np

    out = dict(_drawn_inputs(seed))
    spreads = {}
    factors = {'state_gla': 8.0,
     'lru_br': 8.0,
     'lru_bi': 7.092,
     'gla_bg': 6.551,
     'gla_norm_g': 8.0,
     'norm2_g': 5.157,
     'router_gb': 8.0,
     'router_eb': 8.0,
     'final_g': 2.748}
    for name, (base, spread) in spreads.items():
        noise = np.random.default_rng([zlib.crc32(name.encode()), seed]).standard_normal(out[name].shape)
        drawn = base * np.exp(spread * noise) if base else spread * noise
        out[name] = __import__('jax').numpy.asarray(drawn.astype(out[name].dtype))
    for name, factor in factors.items():
        out[name] = (out[name] * factor).astype(out[name].dtype)
    return out
```

```python
from contextlib import ExitStack

import concourse.bass as bass
from concourse import mybir

F32 = mybir.dt.float32
I32 = mybir.dt.int32
U32 = mybir.dt.uint32
ALU = mybir.AluOpType
ACT = mybir.ActivationFunctionType
AX = mybir.AxisListType

P = 128
EPS = 1e-6
GRID_W = 64
CHUNK = 64
RGLRU_C = 8.0
GLA_TAU = 16.0


def hybrid_step(nc, x_prompt, x_sample, state_lru, state_gla, c, c_ctx, ada_w, ada_b, norm1_g, w_in,
                conv_w, conv_b, lru_wr, lru_br, lru_wi, lru_bi, lru_lam, gla_wg, gla_bg, gla_norm_g,
                w_out, norm2_g, router_gw, router_gb, router_ew, router_eb, exp_w13, exp_w2, final_g,
                y_prompt, y_sample, state_lru_new, state_gla_new):
    D = x_sample.shape[2]
    NS = x_sample.shape[1]
    NP = x_prompt.shape[1]
    N = NS + NP
    KD = D // P
    NT = N // P
    ST = NS // P
    LW = lru_br.shape[2]
    LC = LW // P
    LB = lru_wr.shape[3]
    HEADS, DK, DV = state_gla.shape[3:]
    QK = HEADS * DK
    QT = QK // P
    RANK = gla_wg.shape[2]
    NC = N // CHUNK
    SC = NS // CHUNK
    NG = router_gw.shape[2]
    NE = router_ew.shape[2]
    EG = NE // NG
    DE = exp_w2.shape[2]
    DC = DE // P
    NOV = 2 * N // P - 1
    NU = NE + NOV
    PAD = GRID_W + 3
    PADS = NS // GRID_W * PAD
    XLP = PADS + NP + 3
    assert (D, N, LC, QT, DV, NE, DC, NT) == (1024, 640, 4, 2, P, 16, 2, 5)

    x_s = x_sample[0]
    x_p = x_prompt[0]

    rows_d = nc.dram_tensor("mod_rows", [8 * D], F32).ap()
    h2_d = nc.dram_tensor("h2_rows", [N + 1, D], F32).ap()
    y_d = nc.dram_tensor("expert_rows", [NU * P, D], F32).ap()

    ctx = ExitStack()
    with ctx:
        def sb(name, shape, dt=F32):
            return ctx.enter_context(nc.sbuf_tensor(name, shape, dt))

        def sem(name):
            return ctx.enter_context(nc.semaphore(name))

        W_WORDS = KD * 512
        wring = sb("wring", [P, 3, W_WORDS])
        xres = sb("xres", [P, NT, D])
        mixT = sb("mixT", [P, KD, N])
        r1 = sb("r1", [P, KD * N])
        vtok = sb("vtok", [P, NT * 512])
        qk = sb("qk", [P, 4 * N])
        gd = sb("gd", [P, N])
        TMPW = 12 * N + LC * XLP + LC * N + XLP + 16 * P
        tmp = sb("tmp", [P, TMPW])
        hT = r1[:, :].rearrange("p (k n) -> p k n", k=KD)
        S = r1[:, :].rearrange("p (g c v) -> p g c v", g=4, c=NC)
        v = vtok[:, :].rearrange("p (t n) -> p t n", t=NT)
        q = qk[:, 0:2 * N].rearrange("p (t n) -> p t n", t=2)
        kk = qk[:, 2 * N:4 * N].rearrange("p (t n) -> p t n", t=2)
        osb = qk[:, :].rearrange("p (h n) -> p h n", h=HEADS)
        xhat = tmp[:, 0:NT * D].rearrange("p (t d) -> p t d", t=NT)
        tau = tmp[:, 0:4 * N].rearrange("p (j n) -> p j n", j=4)
        av = tmp[:, 4 * N:8 * N].rearrange("p (j n) -> p j n", j=4)
        ix = tmp[:, 8 * N:12 * N].rearrange("p (j n) -> p j n", j=4)
        o0 = 12 * N
        xlp = tmp[:, o0:o0 + LC * XLP].rearrange("p (c n) -> p c n", c=LC)
        o0 += LC * XLP
        xc = tmp[:, o0:o0 + LC * N].rearrange("p (c n) -> p c n", c=LC)
        o0 += LC * N
        cacc = tmp[:, o0:o0 + XLP]
        o0 += XLP
        lruw = tmp[:, o0:o0 + 16 * P].rearrange("p (w s c n) -> p w s c n", w=2, s=2, c=LC)
        bcum = tmp[:, 0:4 * N].rearrange("p (g n) -> p g n", g=4)
        gt = tmp[:, 4 * N:10 * N].rearrange("p (j n) -> p j n", j=6)
        kdT = tmp[:, 10 * N:14 * N].rearrange("p (g n) -> p g n", g=4)
        qin = tmp[:, 14 * N:18 * N].rearrange("p (g n) -> p g n", g=4)
        att = tmp[:, 18 * N:22 * N].rearrange("p (h n) -> p h n", h=HEADS)
        attb = tmp[:, 22 * N:23 * N]
        sq = kdT
        rows = [[tmp[:, 0:D], tmp[:, D:2 * D], tmp[:, 4 * N:4 * N + D], tmp[:, 4 * N + D:4 * N + 2 * D]],
                [tmp[:, 10 * N:10 * N + D], tmp[:, 10 * N + D:10 * N + 2 * D], qk[:, 0:D], qk[:, D:2 * D]]]
        o0 = 14 * N
        h2 = tmp[:, o0:o0 + 2 * D].rearrange("p (b d) -> p b d", b=2)
        h2T = tmp[:, o0 + 2 * D:o0 + 4 * D].rearrange("p (b k n) -> p b k n", b=2, k=KD)
        mtmp = tmp[:, o0 + 4 * D:o0 + 5 * D]
        e13 = [r1[:, 0:W_WORDS], wring[:, 1, :], wring[:, 2, :], tmp[:, o0:o0 + W_WORDS]]
        e13 = [w.rearrange("p (k f) -> p k f", k=KD) for w in e13]
        mix_flat = mixT[:, :, :].rearrange("p k n -> p (k n)")
        e2 = [vtok[:, 0:DC * D], wring[:, 0, 0:DC * D], wring[:, 0, DC * D:2 * DC * D], mix_flat[:, 0:DC * D]]
        e2 = [w.rearrange("p (k f) -> p k f", k=DC) for w in e2]
        junk = r1[:, :].rearrange("p (t d) -> p t d", t=NT)
        gx = mix_flat[:, DC * D:DC * D + 2 * D].rearrange("p (b d) -> p b d", b=2)
        xgT = tmp[:, 0:2 * D].rearrange("p (b k n) -> p b k n", b=2, k=KD)
        ysb = tmp[:, 10 * N:10 * N + 2 * D].rearrange("p (b d) -> p b d", b=2)
        sact = tmp[:, 10 * N + 2 * D:10 * N + 2 * D + 2 * DE].rearrange("p (b f) -> p b f", b=2)
        act_sb = vtok[:, DC * D:DC * D + 2 * DE].rearrange("p (b f) -> p b f", b=2)
        aT = gd[:, 0:2 * DE].rearrange("p (b k n) -> p b k n", b=2, k=DC)
        yg = wring[:, :, :].rearrange("p s n -> p (s n)")[:, 0:4 * D].rearrange("p (b d) -> p b d", b=4)
        fing = wring[:, 2, 0:D]

        NSM = 89
        sm_in = mix_flat[:, D:D + P]
        adab_in = mix_flat[0:6 * KD, D + P:D + 2 * P]
        smT = sb("smT", [P, NSM])
        adab = sb("adab", [P, 6 * KD])
        cs = sb("cs", [P, KD, 32])
        mod = sb("mod", [P, 6 * KD, 2])
        A1 = sb("A1", [P, KD, 2])
        A2 = sb("A2", [P, 8, KD])
        rows_t = sb("rows_t", [8 * KD, P])
        sg0 = sb("sg0", [P, 4, DV])
        sfin = sb("sfin", [P, 4, DV])
        adrow = [s[:, :, :].rearrange("p g v -> p (g v)") for s in (sg0, sfin)]
        eps = sb("eps", [P, 1])
        zero = sb("zero", [P, P])
        ident = sb("ident", [P, P])
        ones = sb("ones", [P, P])
        before = sb("before", [P, P])
        mask = sb("mask", [P, 2, P])
        wgb = sb("wgb", [2 * RANK, 2 * QK])
        wgd = sb("wgd", [P, KD, 2 * RANK])
        hb = sb("hb", [P, 16])
        lam = sb("lam", [P, 6, 8])
        lfin = sb("lfin", [P, 8])
        lfin_t = sb("lfin_t", [8, P])
        dec = sb("dec", [P, 4, NC])
        st = sb("st", [P, 4, NT])
        rw = sb("rw", [P, KD, NG + NE])
        rbias = sb("rbias", [P, NG + NE])
        free = [0]

        def scratch_of(a, b):
            w = tmp[:, free[0]:free[0] + a * b]
            free[0] += a * b
            assert free[0] <= 2 * D
            return w.rearrange("p (a b) -> p a b", a=a)

        lg = scratch_of(NT, NG + NE)
        r4 = scratch_of(8, NT * NG).rearrange("p a (t e) -> p a t e", t=NT)
        r16 = scratch_of(4, NT * NE).rearrange("p a (t e) -> p a t e", t=NT)
        sel_a = scratch_of(2, P)
        sel_b = scratch_of(2, 2 * NU)
        eid_c = scratch_of(NOV, NE)
        rt = sb("rt", [P, 8, NT])
        w4 = sb("w4", [P, NG])
        io16 = sb("io16", [P, NE])
        io128 = sb("io128", [P, P])
        iou = sb("iou", [P, NU])
        tokid = sb("tokid", [P, NT])
        cnt = sb("cnt", [P, 6, NE])
        eidf = sb("eidf", [P, NOV + 1])
        eidi = sb("eidi", [P, NOV + 1], I32)
        slot_tok = sb("slot_tok", [P, NU], I32)
        slot_gate = sb("slot_gate", [P, NU])
        yidx = sb("yidx", [P, 2 * NT], I32)
        ov_tok = sb("ov_tok", [P, 1], I32)
        ov_gate = sb("ov_gate", [P, 1])

        ps = ctx.enter_context(nc.psum_tensor("ps", [P, 3, 1024], F32))
        ms = ctx.enter_context(nc.psum_tensor("ms", [P, 2, 512], F32))

        order = []
        for j in range(4):
            order += [(f"ad{j}", "A")] + [(f"aT{j - 1}", "D")] * (j > 0)
        order += [("aT3", "D")]
        order += [(f"xT{k}", "AD"[k % 2]) for k in range(KD)]

        def modulation_order(j):
            return [(f"ad{j}", "A"), (f"ad{j + 1}", "A"), (f"aT{j}", "D"), (f"aT{j + 1}", "D")]

        def gates_order(ch, s):
            return [(f"lr{ch}{s}{w}", "A") for w in range(2)]

        order += [(f"xl{t}", "A") for t in range(LC)] + modulation_order(4)
        for n in range(4):
            order += gates_order(n // 2, n % 2) + [(f"yl{n}", "A")]
        order += modulation_order(6)
        order += [(f"k{t}", "A") for t in range(QT)] + [(f"q{t}", "A") for t in range(QT)] + [("gd", "A")]
        order += modulation_order(8)
        for n in range(4):
            order += gates_order(2 + n // 2, n % 2) + [(f"v{n}", "A")]
        order += [("v4", "A")] + modulation_order(10)
        order += [("og0", "A"), ("og1", "A")]
        order += [(f"g{g}", "A") for g in range(4)]
        for g in range(4):
            order += [("og2", "A")] * (g == 0) + [(f"kT{g}", "A"), (f"at{g}0", "D"), (f"at{g}1", "D")]
            order += [("og3", "A")] * (g == 0) + [(f"kvA{g}", "D"), (f"kvB{g}", "D")]
        order += [(f"o{h}", "A") for h in range(HEADS)] + [("ss", "A")] + [(f"rb{h}", "D") for h in range(HEADS)]
        for t in range(NT):
            order += [(f"mx{t}", "D")]
            if t:
                order += [(f"hh{t - 1}", "A")]
        order += [(f"hh{NT - 1}", "A")]
        place = {name: n for n, (name, _) in enumerate(order)}
        RING = 3

        def product(name):
            return ps[:, place[name] % RING, :]

        wi = w_in[0].rearrange("(k p) n -> p k n", p=P)
        aw = ada_w[0].rearrange("(k p) n -> p k n", p=P)
        wo = w_out[0].rearrange("(k p) n -> p k n", p=P)
        QK0, V0, OG0, GD0 = 2 * LW, 2 * LW + 2 * QK, 2 * LW + 2 * QK + HEADS * DV, 2 * LW + 2 * QK + 2 * HEADS * DV
        pieces = [(f"a{j}", aw[:, :, 512 * j:512 * j + 512]) for j in range(4)]
        for n, (name, col) in enumerate((("xl", 0), ("yl", LW), ("qk", QK0), ("v", V0), ("og", OG0))):
            pieces += [(name, wi[:, :, col:col + 512])]
            if n < 4:
                pieces += [(f"a{j}", aw[:, :, 512 * j:512 * j + 512]) for j in (2 * n + 4, 2 * n + 5)]
        pieces += [(f"wo{j}", wo[:, :, 512 * j:512 * j + 512]) for j in range(2)]
        piece = {name: n for n, (name, _) in enumerate(pieces)}

        last_use = {"qk": "q1", "xl": "xl3", "yl": "yl3", "v": "v4", "og": "og3"}

        def weights(name):
            return wring[:, piece[name] % 3, :].rearrange("p (k n) -> p k n", k=KD)

        small_in = sem("small_in")
        bias_in = sem("bias_in")
        x_in = [sem(f"x_in{t}") for t in range(NT)]
        gdw_in = sem("gdw_in")
        lruw_in = sem("lruw_in")
        piece_in = [sem(f"piece_in{i}") for i in range(3)]
        consts = sem("consts")
        smt_ready = sem("smt_ready")
        smt_out = sem("smt_out")
        cs_zero = sem("cs_zero")
        cs_ready = sem("cs_ready")
        mod_out = sem("mod_out")
        xhat_ready = sem("xhat_ready")
        product_ready = sem("product_ready")
        took = {"A": sem("act_took"), "D": sem("dve_took")}
        sums = sem("sums")
        means = sem("means")
        roots = sem("roots")
        act_chain = sem("act_chain")
        dve_chain = sem("dve_chain")
        pool_chain = sem("pool_chain")
        xlp_zero = sem("xlp_zero")
        lam_exp = sem("lam_exp")
        lam_abs = sem("lam_abs")
        lam_ready = sem("lam_ready")
        conv_ready = sem("conv_ready")
        lru_act = sem("lru_act")
        lru_sqrt = sem("lru_sqrt")
        lru_done = sem("lru_done")
        att_zero = sem("att_zero")
        scan_mask = sem("scan_mask")
        zmin = sem("zmin")
        zlog = sem("zlog")
        bready = sem("bready")
        diffs = sem("diffs")
        exps = sem("exps")
        qk_ready = sem("qk_ready")
        kd_ready = sem("kd_ready")
        qin_ready = sem("qin_ready")
        rd_ready = sem("rd_ready")
        sg_in = sem("sg_in")
        att_ready = sem("att_ready")
        oroot = sem("oroot")
        orms = sem("orms")
        mix_ready = sem("mix_ready")
        rowsT = sem("rowsT")
        rows_t_out = sem("rows_t_out")
        rows_out = sem("rows_out")
        rows_in = [sem(f"rows_in{i}") for i in range(2)]
        h2_ready = sem("h2_ready")
        h2_out = [sem(f"h2_out{i}") for i in range(2)]
        zrow_out = sem("zrow_out")
        lfin_ready = sem("lfin_ready")
        lfinT = sem("lfinT")
        lfin_t_out = sem("lfin_t_out")
        outs = sem("outs")
        logits_ready = sem("logits_ready")
        gexp = sem("gexp")
        gready = sem("gready")
        eexp = sem("eexp")
        eready = sem("eready")
        choice = sem("choice")
        ranks = sem("ranks")
        onehots = sem("onehots")
        onehots_used = sem("onehots_used")
        tables = sem("tables")
        routed = sem("routed")
        e13_in = [sem(f"e13_in{i}") for i in range(4)]
        e2_in = [sem(f"e2_in{i}") for i in range(4)]
        gx_in = [sem(f"gx_in{i}") for i in range(2)]
        x_turned = sem("x_turned")
        x_taken = sem("x_taken")
        hid = sem("hid")
        silu = sem("silu")
        act_ready = sem("act_ready")
        a_turned = sem("a_turned")
        a_taken = sem("a_taken")
        y_done = sem("y_done")
        y_taken = sem("y_taken")
        y_out = [sem(f"y_out{i}") for i in range(2)]
        moe_done = sem("moe_done")
        ov = {n: sem("ov_" + n) for n in ("tok", "w", "gx", "xT", "xg", "hid", "silu", "act", "aT", "at", "y", "yt", "out", "sc")}
        ov_turns = sem("ov_turns")
        yg_in = [sem(f"yg_in{i}") for i in range(2)]
        yg_used = sem("yg_used")
        fg_in = sem("fg_in")
        ready_out = sem("ready_out")

        sm_parts = [(c, KD), (c_ctx.rearrange("(a n) -> a n", a=1), KD), (norm1_g, KD), (norm2_g, KD), (conv_w[0], 4 * LC),
                    (conv_b, LC), (lru_br[0], 8), (lru_bi[0], 8), (lru_lam[0], 8), (gla_bg[0], 4),
                    (state_lru[0, 0], 8), (gla_norm_g, 1)]
        at, off = [], 0
        for _, n in sm_parts:
            at.append(off)
            off += n
        assert off == NSM
        C0, CX0, N1, N2, CW, CB, BR, BI, LAM, BG, H0, GN = at
        SMALL = 16 * len(sm_parts)
        BIASES = 16 * 6

        def wait_piece(eng, name):
            n = piece[name]
            eng.wait_ge(piece_in[n % 3], 16 * (n // 3 + 1))

        def count(name):
            who = order[place[name]][1]
            return who, sum(w == who for _, w in order[:place[name] + 1])

        def wait_taken(eng, name):
            who, n = count(name)
            eng.wait_ge(took[who], n)

        def halves(ap):
            return ap[:, 0:NS], ap[:, NS:N]

        block = ctx.enter_context(nc.Block())

        @block.sync
        def _(sp):
            def load_piece(name):
                n = piece[name]
                if n >= 3:
                    old = pieces[n - 3][0]
                    use = f"ad{old[1:]}" if old[0] == "a" else last_use[old]
                    sp.wait_ge(product_ready, place[use] + 1)
                sp.dma_start(wring[:, n % 3, :].rearrange("p (k n) -> p k n", k=KD), pieces[n][1]) \
                    .then_inc(piece_in[n % 3], 16)

            for n in range(3):
                load_piece(pieces[n][0])
            for t in range(NT):
                src = x_s[t * P:t * P + P, :] if t < ST else x_p[(t - ST) * P:(t - ST) * P + P, :]
                sp.dma_start(xres[:, t, :], src).then_inc(x_in[t], 16)
            for n in range(3, 6):
                load_piece(pieces[n][0])
            sp.dma_start(wgd[:, :, :], wi[:, :, GD0:GD0 + 2 * RANK]).then_inc(gdw_in, 16)
            sp.wait_ge(consts, 2)
            sp.dma_start(h2_d[N, :].rearrange("(k n) -> k n", n=P), zero[0:KD, :]).then_inc(zrow_out, 16)
            for s in range(2):
                sp.dma_start(wgb[s * RANK:(s + 1) * RANK, s * QK:(s + 1) * QK], gla_wg[0, s]).then_inc(bias_in, 16)
            sp.dma_start(rbias[:, 0:NG], router_gb.to_broadcast([P, NG])).then_inc(bias_in, 16)
            sp.dma_start(rbias[:, NG:], router_eb.to_broadcast([P, NE])).then_inc(bias_in, 16)
            sp.dma_start(rw[:, :, 0:NG], router_gw[0].rearrange("(k p) n -> p k n", p=P)).then_inc(bias_in, 16)
            sp.dma_start(rw[:, :, NG:], router_ew[0].rearrange("(k p) n -> p k n", p=P)).then_inc(bias_in, 16)
            for wn, src in enumerate((lru_wr, lru_wi)):
                for s in range(2):
                    blocks = src[0, s].rearrange("(c h) a b -> h a c b", h=2)
                    for half in range(2):
                        sp.dma_start(lruw[half * LB:(half + 1) * LB, wn, s, :, half * LB:(half + 1) * LB],
                                     blocks[half]).then_inc(lruw_in, 16)
            for n in range(6, 17):
                load_piece(pieces[n][0])
                if n >= 8:
                    u = n - 8
                    sp.dma_start(y_d[(NE + u) * P:(NE + u + 1) * P, :].rearrange("p (k n) -> p k n", n=P),
                                 zero[:, :].rearrange("p (a n) -> p a n", a=1).to_broadcast([P, KD, P])).then_inc(zrow_out, 16)
            wait_taken(sp, "aT11")
            for s in range(2):
                for t in range(QT):
                    sp.dma_start(sg0[:, 2 * t + s, :], state_gla[0, 0, s, 2 * t:2 * t + 2].rearrange("h k v -> (h k) v")) \
                        .then_inc(sg_in, 16)
            sp.wait_ge(rows_t_out, 1)
            sp.dma_start(rows_d.rearrange("(r n) -> r n", n=P), rows_t[:, :]).then_inc(rows_out, 16)
            load_piece("wo0")
            load_piece("wo1")
            sp.wait_ge(rows_out, 16)
            sp.wait_ge(qk_ready, 4)
            wait_taken(sp, "at31")
            wait_taken(sp, "kT3")

            def load_row(seq, kind):
                i = 4 * seq + kind
                sp.dma_start(rows[seq][kind], rows_d[i * D:(i + 1) * D].rearrange("(a n) -> a n", a=1).to_broadcast([P, D])) \
                    .then_inc(rows_in[seq], 16)

            for kind in range(4):
                load_row(0, kind)
            wait_taken(sp, "kvB3")
            for s in range(2):
                for t in range(QT):
                    sp.dma_start(state_gla_new[0, 0, s, 2 * t:2 * t + 2].rearrange("h k v -> (h k) v"), sfin[:, 2 * t + s, :]) \
                        .then_inc(outs, 16)
            wait_taken(sp, "rb3")
            sp.wait_ge(mix_ready, HEADS)
            for kind in range(4):
                load_row(1, kind)
            sp.wait_ge(lfin_t_out, 1)
            sp.dma_start(state_lru_new[0, 0].rearrange("s (c n) -> (s c) n", n=P), lfin_t[:, :]).then_inc(outs, 16)

            def load13(u):
                w = exp_w13[0, u].rearrange("(k p) f -> p k f", p=P)
                sp.dma_start(e13[u % 4], w).then_inc(e13_in[u % 4], 16)

            def load2(u):
                w = exp_w2[0, u].rearrange("(k p) f -> p k f", p=P)
                sp.dma_start(e2[u % 4], w).then_inc(e2_in[u % 4], 16)

            load13(0)
            load2(0)
            load13(1)
            for t in range(NT):
                sp.wait_ge(h2_ready, t + 1)
                sp.dma_start(h2_d[t * P:(t + 1) * P, :], h2[:, t % 2, :]).then_inc(h2_out[t % 2], 16)
            wait_taken(sp, "mx4")
            load2(1)
            load13(2)
            load2(2)
            sp.wait_ge(logits_ready, NT)
            for i in range(2):
                sp.wait_ge(h2_out[i], 16 * ((NT - i + 1) // 2))
            load13(3)
            load2(3)
            for u in range(4, NE):
                sp.wait_ge(hid, u - 3)
                load13(u)
                sp.wait_ge(y_done, 2 * (u - 3))
                load2(u)

            sp.wait_ge(moe_done, 1)
            n_over = sp.value_load(eidi[0:1, NOV:NOV + 1], min_val=0, max_val=NOV)
            with sp.Fori(0, NOV) as i:
                with sp.If(n_over > i):
                    e = sp.value_load(eidi[0:1, bass.ds(i, 1)], min_val=0, max_val=NE - 1)
                    sp.dma_start(e13[0], exp_w13[0, bass.ds(e, 1)].rearrange("a (k p) f -> p (a k) f", p=P)).then_inc(ov["w"], 16)
                    sp.dma_start(e2[0], exp_w2[0, bass.ds(e, 1)].rearrange("a (k p) f -> p (a k) f", p=P)).then_inc(ov["w"], 16)
                    sp.wait_ge(ov["yt"], i + 1)
                    sp.dma_start(y_d[bass.ds((i + NE) * P, P), :], ysb[:, 0, :]).then_inc(ov["out"], 16)
                    sp.wait_ge(ov["out"], (i + 1) * 16)
                    sp.sem_inc(ov_turns, 1)
                sp.nop()
            sp.dma_start(fing, final_g.rearrange("(a n) -> a n", a=1).to_broadcast([P, D])).then_inc(fg_in, 16)
            for t in range(NT):
                sp.wait_ge(ready_out, t + 1)
                dst = y_sample[0, t * P:t * P + P, :] if t < ST else y_prompt[0, (t - ST) * P:(t - ST) * P + P, :]
                sp.dma_start(dst, xres[:, t, :]).then_inc(outs, 16)
            sp.wait_ge(outs, 16 * (4 + 1 + NT))

        @block.gpsimd
        def _(pool):
            n_chain = [0]

            def link(ins):
                n_chain[0] += 1
                ins.then_inc(pool_chain, 1)
                pool.wait_ge(pool_chain, n_chain[0])

            nc.gpsimd.memset(cs[:, :, :], 0.0).then_inc(cs_zero, 1)
            link(nc.gpsimd.memset(ident[:, :], 0.0))
            nc.gpsimd.affine_select(out=ident[:, :], in_=ident[:, :], compare_op=ALU.not_equal, fill=1.0, base=0,
                                    pattern=[[-1, P]], channel_multiplier=1).then_inc(consts, 1)
            nc.gpsimd.memset(eps[:, :], EPS)
            nc.gpsimd.memset(zero[:, :], 0.0)
            nc.gpsimd.memset(wgb[:, :], 0.0)
            link(nc.gpsimd.memset(ones[:, :], 1.0))
            nc.gpsimd.memset(lruw[:, :, :, :, :].rearrange("p w s c n -> p (w s c n)"), 0.0).then_inc(consts, 1)
            nc.gpsimd.memset(xlp[:, :, 0:PADS].rearrange("p c (r w) -> p c r w", w=PAD)[:, :, :, 0:2], 0.0)
            nc.gpsimd.memset(xlp[:, :, 0:PADS].rearrange("p c (r w) -> p c r w", w=PAD)[:, :, :, PAD - 1:PAD], 0.0)
            nc.gpsimd.memset(xlp[:, :, PADS:PADS + 2], 0.0)
            nc.gpsimd.memset(xlp[:, :, XLP - 1:XLP], 0.0).then_inc(xlp_zero, 1)
            nc.gpsimd.affine_select(out=before[:, :], in_=ones[:, :], compare_op=ALU.is_gt, fill=0.0, base=0,
                                    pattern=[[1, P]], channel_multiplier=-1)
            nc.gpsimd.affine_select(out=mask[:, 0, :], in_=ones[:, :], compare_op=ALU.is_ge, fill=0.0, base=0,
                                    pattern=[[1, P]], channel_multiplier=-1)
            link(nc.gpsimd.affine_select(out=mask[:, 1, :], in_=ones[:, :], compare_op=ALU.is_ge, fill=0.0, base=0,
                                         pattern=[[-1, P]], channel_multiplier=1))
            link(nc.gpsimd.memset(mask[0:CHUNK, 0, CHUNK:P], 0.0))
            link(nc.gpsimd.memset(mask[CHUNK:P, 1, 0:CHUNK], 0.0))
            nc.gpsimd.iota(io16[:, :], pattern=[[1, NE]], base=0, channel_multiplier=0, allow_small_or_imprecise_dtypes=True)
            nc.gpsimd.iota(io128[:, :], pattern=[[1, P]], base=0, channel_multiplier=0, allow_small_or_imprecise_dtypes=True)
            nc.gpsimd.iota(iou[:, :], pattern=[[1, NU]], base=0, channel_multiplier=0, allow_small_or_imprecise_dtypes=True)
            nc.gpsimd.iota(w4[:, :], pattern=[[-1, NG]], base=NG, channel_multiplier=0, allow_small_or_imprecise_dtypes=True)
            nc.gpsimd.iota(tokid[:, :], pattern=[[P, NT]], base=-N, channel_multiplier=1, allow_small_or_imprecise_dtypes=True) \
                .then_inc(consts, 1)
            pool.wait_ge(lru_done, 2)
            nc.gpsimd.memset(attb[:, :], 0.0)
            nc.gpsimd.memset(tmp[:, 18 * N:22 * N], 0.0).then_inc(att_zero, 1)
            wait_taken(pool, "g3")
            link(nc.gpsimd.memset(gd[:, :], 1.0))
            nc.gpsimd.memset(gd[:, :].rearrange("p (c i) -> p c i", i=CHUNK)[:, :, 0:1], 0.0).then_inc(scan_mask, 1)
            wait_taken(pool, "q1")
            for g in range(4):
                r = 3 * (g % 2)
                last = CHUNK - 1 if g % 2 == 0 else 0
                pool.wait_ge(exps, g + 1)
                nc.gpsimd.tensor_tensor(gt[:, r + 2, :], gt[:, r + 2, :], kk[:, g // 2, :], ALU.mult).then_inc(kd_ready, 1)
                link(nc.gpsimd.tensor_copy(dec[:, g, :], qin[:, g, :].rearrange("p (c i) -> p c i", i=CHUNK)[:, :, last]))
                nc.gpsimd.tensor_tensor(qin[:, g, :], qin[:, g, :], q[:, g // 2, :], ALU.mult).then_inc(qin_ready, 1)

            def gather(u):
                b = u % 2
                if u >= 2:
                    pool.wait_ge(x_turned, u - 1)
                pool.indirect_dma_start(gx[:, b, :], None, h2_d[:, :],
                                        bass.IndirectOffsetOnAxis(ap=slot_tok[:, u:u + 1].bitcast(U32), axis=0)) \
                    .then_inc(gx_in[b], 16)

            pool.wait_ge(routed, 1)
            for i in range(2):
                pool.wait_ge(h2_out[i], 16 * ((NT - i + 1) // 2))
            pool.wait_ge(zrow_out, 16 * (1 + NOV))
            for u in range(NE):
                gather(u)
            pool.wait_ge(moe_done, 1)
            n_over = pool.value_load(eidi[0:1, NOV:NOV + 1], min_val=0, max_val=NOV)
            with pool.Fori(0, NOV) as i:
                with pool.If(n_over > i):
                    pool.wait_ge(ov["tok"], i + 1)
                    pool.sem_inc(ov_turns, 1)
                    pool.indirect_dma_start(gx[:, 0, :], None, h2_d[:, :],
                                            bass.IndirectOffsetOnAxis(ap=ov_tok[:, 0:1].bitcast(U32), axis=0)) \
                        .then_inc(ov["gx"], 16)
                    pool.wait_ge(ov["out"], (i + 1) * 16)
                    pool.sem_inc(ov_turns, 1)
                pool.nop()
            for i in range(2):
                pool.wait_ge(y_out[i], 16 * NE // 2)
            for t in range(NT):
                if t >= 2:
                    pool.wait_ge(yg_used, t - 1)
                for j in range(2):
                    pool.indirect_dma_start(yg[:, 2 * (t % 2) + j, :], None, y_d[:, :],
                                            bass.IndirectOffsetOnAxis(ap=yidx[:, j * NT + t:j * NT + t + 1].bitcast(U32), axis=0)) \
                        .then_inc(yg_in[t % 2], 16)

        @block.scalar
        def _(act):
            A = nc.scalar.activation
            n_chain = [0]

            def chain(ins):
                n_chain[0] += 1
                ins.then_inc(act_chain, 1)

            def settle():
                act.wait_ge(act_chain, n_chain[0])

            def ready(name):
                act.wait_ge(product_ready, place[name] + 1)
                return product(name)

            for (src, n), r in zip(sm_parts, at):
                width = P if n > 1 else src.shape[-1]
                if len(src.shape) == 2:
                    src = src.rearrange("a (b n) -> (a b) n", n=width)
                act.dma_start(sm_in[r:r + n, :], src).then_inc(small_in, 16)
            act.dma_start(adab_in, ada_b.rearrange("a (m n) -> (a m) n", n=P)).then_inc(small_in, 16)
            act.wait_ge(cs_zero, 1)
            act.wait_ge(smt_out, 1)
            A(cs[:, :, 0], smT[:, C0:C0 + KD], ACT.Silu)
            A(cs[:, :, 1], smT[:, CX0:CX0 + KD], ACT.Silu).then_inc(cs_ready, 1)
            for t in range(NT):
                act.wait_ge(x_in[t], 16)
                i = A(junk[:, t, :], xres[:, t, :], ACT.Square, accum_out=st[:, 0, t:t + 1])
            i.then_inc(sums, 1)
            chain(A(lam[:, 0, :], smT[:, LAM:LAM + 8], ACT.Abs))
            settle()
            A(lam[:, 1, :], lam[:, 0, :], ACT.Exp, scale=-1.0).then_inc(lam_exp, 1)
            act.wait_ge(means, 1)
            A(st[:, 2, :], st[:, 1, :], ACT.Sqrt).then_inc(roots, 1)
            chain(A(hb[:, :], smT[:, BR:BR + 16], ACT.Copy, scale=0.5))
            def take_mod(j):
                if j >= 2:
                    act.wait_ge(product_ready, place[f"aT{j - 2}"] + 1)
                A(adrow[j % 2], ready(f"ad{j}")[:, 0:512], ACT.Copy).then_inc(took["A"], 1)

            for j in range(4):
                take_mod(j)
            act.wait_ge(mod_out, 1)
            for k in range(0, KD, 2):
                src = ready(f"xT{k}")
                A(hT[:, k, 0:NS], src[:, 0:NS], ACT.Identity, bias=mod[:, k, 0:1], scale=A1[:, k, 0:1])
                A(hT[:, k, NS:N], src[:, NS:N], ACT.Identity, bias=mod[:, k, 1:2], scale=A1[:, k, 1:2]).then_inc(took["A"], 1)
            act.wait_ge(xlp_zero, 1)
            for t in range(LC):
                src = ready(f"xl{t}")
                A(xlp[:, t, 0:PADS].rearrange("p (r w) -> p r w", w=PAD)[:, :, 2:PAD - 1],
                  src[:, 0:NS].rearrange("p (r w) -> p r w", w=GRID_W), ACT.Copy)
                A(xlp[:, t, PADS + 2:XLP - 1], src[:, NS:N], ACT.Copy).then_inc(took["A"], 1)
            take_mod(4)
            take_mod(5)
            act.wait_ge(lam_ready, 1)
            for h in range(2):
                if h:
                    act.wait_ge(lru_done, h)
                for j in range(4):
                    ch, s = 2 * h + j // 2, j % 2
                    for w, dst in enumerate((tau, ix)):
                        b = 8 * w + 4 * s + ch
                        A(dst[:, j, :], ready(f"lr{ch}{s}{w}")[:, 0:N], ACT.Tanh, bias=hb[:, b:b + 1], scale=0.5) \
                            .then_inc(took["A"], 1)
                    if h == 0:
                        A(mixT[:, j, :], ready(f"yl{j}")[:, 0:N], ACT.Gelu_apprx_tanh).then_inc(took["A"], 1)
                    else:
                        A(v[:, j, :], ready(f"v{j}")[:, 0:512], ACT.Copy).then_inc(took["A"], 1)
                act.wait_ge(took["A"], count(f"lr{2 * h + 1}11")[1])
                for j in range(4):
                    m = 4 * (j % 2) + 2 * h + j // 2
                    A(av[:, j, :], tau[:, j, :], ACT.Exp, bias=lam[:, 3, m:m + 1], scale=lam[:, 3, m:m + 1])
                    chain(A(tau[:, j, :], tau[:, j, :], ACT.Tanh, bias=lam[:, 4, m:m + 1], scale=lam[:, 4, m:m + 1]))
                settle()
                for j in range(4):
                    A(tau[:, j, :], tau[:, j, :], ACT.Sqrt, scale=0.25).then_inc(lru_sqrt, 1)
                if h == 0:
                    take_mod(6)
                    take_mod(7)
                    for t in range(QT):
                        A(kk[:, t, :], ready(f"k{t}")[:, 0:N], ACT.Copy).then_inc(took["A"], 1)
                    for t in range(QT):
                        A(q[:, t, :], ready(f"q{t}")[:, 0:N], ACT.Copy, scale=DK ** -0.5).then_inc(took["A"], 1)
                    A(gd[0:2 * RANK, :], ready("gd")[0:2 * RANK, 0:N], ACT.Copy).then_inc(took["A"], 1)
                    take_mod(8)
                    take_mod(9)
            A(v[:, 4, :], ready("v4")[:, 0:512], ACT.Copy).then_inc(took["A"], 1)
            take_mod(10)
            take_mod(11)
            for h in range(2):
                A(mixT[:, LC + h, :], ready(f"og{h}")[:, 0:N], ACT.Silu).then_inc(took["A"], 1)
            act.wait_ge(lru_done, 2)
            for g in range(4):
                b = BG + 2 * (g % 2) + g // 2
                A(bcum[:, g, :], ready(f"g{g}")[:, 0:N], ACT.Identity, bias=smT[:, b:b + 1]).then_inc(took["A"], 1)
            for g in range(4):
                act.wait_ge(took["A"], count(f"g{g}")[1])
                chain(A(gt[:, g, :], bcum[:, g, :], ACT.Abs))
            settle()
            for g in range(4):
                chain(A(gt[:, g, :], gt[:, g, :], ACT.Exp, scale=-1.0))
            settle()
            for g in range(4):
                A(gt[:, g, :], gt[:, g, :], ACT.Ln, bias=1.0).then_inc(zlog, 1)

            def exponentials(g):
                r = 3 * (g % 2)
                act.wait_ge(diffs, g + 1)
                A(qin[:, g, :], bcum[:, g, :], ACT.Exp, scale=1 / GLA_TAU)
                chain(A(gt[:, r + 1, :], gt[:, r, :], ACT.Exp, scale=-1 / GLA_TAU))
                A(gt[:, r, :], gt[:, r, :], ACT.Exp, scale=1 / GLA_TAU)
                A(gt[:, r + 2, :], gt[:, r + 2, :], ACT.Exp, scale=1 / GLA_TAU).then_inc(exps, 1)

            def take_kT(g):
                A(kdT[:, g, :], ready(f"kT{g}")[:, 0:N], ACT.Copy).then_inc(took["A"], 1)

            exponentials(0)
            A(mixT[:, LC + 2, :], ready("og2")[:, 0:N], ACT.Copy).then_inc(took["A"], 1)
            exponentials(1)
            take_kT(0)
            A(mixT[:, LC + 3, :], ready("og3")[:, 0:N], ACT.Copy).then_inc(took["A"], 1)
            exponentials(2)
            take_kT(1)
            exponentials(3)
            take_kT(2)
            act.wait_ge(took["A"], count("og3")[1])
            for h in range(2, HEADS):
                chain(A(mixT[:, LC + h, :], mixT[:, LC + h, :], ACT.Silu))
            take_kT(3)
            settle()
            for h in range(HEADS):
                src = ready(f"o{h}")
                if h == 0:
                    wait_taken(act, "kvB3")
                A(osb[:, h, :], src[:, 0:N], ACT.Copy)
                A(sq[:, h, :], src[:, 0:N], ACT.Square).then_inc(took["A"], 1)
            act.wait_ge(bready, 4)
            A(gd[:, :], ready("ss")[:, 0:N], ACT.Sqrt, bias=eps[:, 0:1], scale=1 / DV).then_inc(took["A"], 1)
            def take_rows(t):
                if t >= 2:
                    act.wait_ge(logits_ready, t - 1)
                A(h2T[:, t % 2, :, :].rearrange("p k n -> p (k n)"), ready(f"hh{t}"), ACT.Copy).then_inc(took["A"], 1)

            for t in range(NT):
                if t:
                    take_rows(t - 1)
                act.wait_ge(rd_ready, t + 1)
                A(mtmp, xres[:, t, :], ACT.Square, accum_out=st[:, 3, t:t + 1]).then_inc(sums, 1)
                act.wait_ge(means, 2 + t)
                A(rt[:, 1, t:t + 1], rt[:, 0, t:t + 1], ACT.Sqrt).then_inc(roots, 1)
            take_rows(NT - 1)
            act.wait_ge(gready, 1)
            A(r4[:, 1, :, :], r4[:, 0, :, :], ACT.Exp).then_inc(gexp, 1)
            act.wait_ge(eready, 1)
            A(r4[:, 4, :, :], r4[:, 3, :, :], ACT.Exp).then_inc(eexp, 1)

            def silu_of(u):
                act.wait_ge(hid, u + 1)
                if u >= 2:
                    act.wait_ge(act_ready, u - 1)
                A(sact[:, u % 2, :], ms[:, u % 2, 0:DE], ACT.Silu).then_inc(silu, 1)

            silu_of(0)
            for u in range(NE):
                if u + 1 < NE:
                    silu_of(u + 1)
                b = u % 2
                if u >= 2:
                    act.wait_ge(y_out[b], 16 * (u // 2))
                for h in range(2):
                    act.wait_ge(y_done, 2 * u + h + 1)
                    A(ysb[:, b, h * 512:(h + 1) * 512], ps[:, 2, h * 512:(h + 1) * 512], ACT.Copy).then_inc(y_taken, 1)
                act.wait_ge(y_taken, 2 * u + 2)
                act.dma_start(y_d[u * P:(u + 1) * P, :], ysb[:, b, :]).then_inc(y_out[b], 16)
            for i in range(2):
                act.wait_ge(y_out[i], 16 * NE // 2)
            n_over = act.value_load(eidi[0:1, NOV:NOV + 1], min_val=0, max_val=NOV)
            act.sem_inc(moe_done, 1)
            with act.Fori(0, NOV) as i:
                with act.If(n_over > i):
                    act.wait_ge(ov["hid"], i + 1)
                    A(sact[:, 0, :], ms[:, 0, 0:DE], ACT.Silu).then_inc(ov["silu"], 1)
                    act.wait_ge(ov["y"], i + 1)
                    A(ysb[:, 0, :], ps[:, 2, :], ACT.Copy).then_inc(ov["yt"], 1)
                    act.wait_ge(ov["out"], (i + 1) * 16)
                    act.sem_inc(ov_turns, 1)
                act.nop()
            for t in range(NT):
                act.wait_ge(rd_ready, NT + t + 1)
                A(yg[:, 2 * (t % 2) + 1, :], xres[:, t, :], ACT.Square, accum_out=st[:, 0, t:t + 1]).then_inc(sums, 1)
                act.wait_ge(means, 2 + NT + t)
                A(st[:, 2, t:t + 1], st[:, 1, t:t + 1], ACT.Sqrt).then_inc(roots, 1)

        @block.tensor
        def _(pe):
            mm = nc.tensor.matmul

            def start(name):
                n = place[name]
                if n >= RING:
                    wait_taken(pe, order[n - RING][0])
                return product(name)

            def wide(dst, lhsT, rhs, first, last):
                for d, r in zip(halves(dst), halves(rhs)):
                    i = mm(d, lhsT, r, start=first, stop=last)
                return i

            pe.wait_ge(consts, 1)
            pe.wait_ge(small_in, SMALL + 16)
            nc.tensor.transpose(ms[:, 0, 0:NSM], sm_in[0:NSM, :], ident[0:NSM, 0:NSM])
            nc.tensor.transpose(ms[:, 0, P:P + 6 * KD], adab_in, ident[0:6 * KD, 0:6 * KD]).then_inc(smt_ready, 1)

            def modulation(j):
                dst = start(f"ad{j}")
                wait_piece(pe, f"a{j}")
                w = weights(f"a{j}")
                for k in range(KD):
                    r = 32 * (k % 4)
                    i = mm(dst[r:r + 32, 0:512], cs[:, k, :], w[:, k, :], start=(k < 4), stop=(k >= 4), skip_group_check=True)
                i.then_inc(product_ready, 1)

            def turn_modulation(j):
                dst = start(f"aT{j}")
                wait_taken(pe, f"ad{j}")
                for m in range(4):
                    i = nc.tensor.transpose(dst[:, m * P:(m + 1) * P], adrow[j % 2][:, m * P:(m + 1) * P], ident[:, :])
                i.then_inc(product_ready, 1)

            def two_modulations(j):
                for f in (modulation, turn_modulation):
                    f(j)
                    f(j + 1)

            pe.wait_ge(cs_ready, 1)
            for j in range(4):
                modulation(j)
                if j:
                    turn_modulation(j - 1)
            turn_modulation(3)
            pe.wait_ge(xhat_ready, 1)
            for k in range(KD):
                dst = start(f"xT{k}")
                for t in range(NT):
                    i = nc.tensor.transpose(dst[:, t * P:(t + 1) * P], xhat[:, t, k * P:(k + 1) * P], ident[:, :])
                i.then_inc(product_ready, 1)
            wait_taken(pe, f"xT{KD - 1}")
            wait_taken(pe, f"xT{KD - 2}")

            def project(name, w, col, rows=P):
                dst = start(name)
                for k in range(KD):
                    i = wide(dst[0:rows, :], w[:, k, col:col + rows], hT[:, k, :], k == 0, k == KD - 1)
                i.then_inc(product_ready, 1)
                return i

            def gates(ch, s):
                pe.wait_ge(conv_ready, ch + 1)
                for w in range(2):
                    wide(start(f"lr{ch}{s}{w}"), lruw[:, w, s, ch, :], xc[:, ch, :], True, True).then_inc(product_ready, 1)

            def values(t):
                dst = start(f"v{t}")
                w = weights("v")
                for k in range(KD):
                    i = mm(dst[:, 0:512], hT[:, k, t * P:(t + 1) * P], w[:, k, :], start=(k == 0), stop=(k == KD - 1))
                i.then_inc(product_ready, 1)

            wait_piece(pe, "xl")
            for t in range(LC):
                project(f"xl{t}", weights("xl"), t * P)
            two_modulations(4)
            pe.wait_ge(lruw_in, 16 * 8)
            wait_piece(pe, "yl")
            for n in range(4):
                gates(n // 2, n % 2)
                project(f"yl{n}", weights("yl"), n * P)
            two_modulations(6)
            wait_piece(pe, "qk")
            for t in range(QT):
                project(f"k{t}", weights("qk"), QK + t * P)
            for t in range(QT):
                project(f"q{t}", weights("qk"), t * P)
            pe.wait_ge(gdw_in, 16)
            project("gd", wgd, 0, 2 * RANK)
            two_modulations(8)
            wait_piece(pe, "v")
            for n in range(4):
                gates(2 + n // 2, n % 2)
                values(n)
            values(4)
            two_modulations(10)
            wait_piece(pe, "og")
            for h in range(2):
                project(f"og{h}", weights("og"), h * P)
            pe.wait_ge(bias_in, BIASES)
            wait_taken(pe, "gd")
            for g in range(4):
                col = (g % 2) * QK + (g // 2) * P
                wide(start(f"g{g}"), wgb[:, col:col + P], gd[0:2 * RANK, :], True, True).then_inc(product_ready, 1)
            pe.wait_ge(mod_out, 2)
            nc.tensor.transpose(ms[0:8 * KD, 0, 0:P], A2[:, :, :].rearrange("p a k -> p (a k)"), ident[:, :]).then_inc(rowsT, 1)
            pe.wait_ge(lfin_ready, 8)
            nc.tensor.transpose(ms[0:8, 0, P:2 * P], lfin[:, :], ident[:, :]).then_inc(lfinT, 1)
            for g in range(4):
                r = 3 * (g % 2)
                tt = g // 2
                if g == 0:
                    project("og2", weights("og"), 2 * P)
                pe.wait_ge(kd_ready, g + 1)
                dst = start(f"kT{g}")
                for t in range(NT):
                    i = nc.tensor.transpose(dst[:, t * P:(t + 1) * P], gt[:, r + 2, t * P:(t + 1) * P], ident[:, :])
                i.then_inc(product_ready, 1)
                pe.wait_ge(qk_ready, g + 1)
                for hh in range(2):
                    dst = start(f"at{g}{hh}")
                    rows_h = slice(hh * DK, (hh + 1) * DK)
                    for t in range(NT):
                        cols = slice(t * P, (t + 1) * P)
                        i = mm(dst[:, cols], gt[rows_h, r + 1, cols], gt[rows_h, r, cols], start=True, stop=True)
                    i.then_inc(product_ready, 1)
                if g == 0:
                    project("og3", weights("og"), 3 * P)
                wait_taken(pe, f"kT{g}")
                for name, chunks in ((f"kvA{g}", range(SC)), (f"kvB{g}", range(SC, NC))):
                    dst = start(name)
                    for cn in chunks:
                        half = slice((cn % 2) * CHUNK, (cn % 2 + 1) * CHUNK)
                        col = (cn % 2) * 512 + (cn - chunks[0]) // 2 * DV
                        t = cn // 2
                        for hh in range(2):
                            h = 2 * tt + hh
                            i = mm(dst[hh * DK:(hh + 1) * DK, col:col + DV],
                                   kdT[half, g, t * P + hh * DK:t * P + (hh + 1) * DK], v[half, t, h * DV:(h + 1) * DV],
                                   start=True, stop=True)
                    i.then_inc(product_ready, 1)
            pe.wait_ge(sg_in, 16 * 4)
            wait_taken(pe, "kvB3")
            pe.wait_ge(qin_ready, 4)
            for h in range(HEADS):
                tt, hh = h // 2, h % 2
                rows_h = slice(hh * DK, (hh + 1) * DK)
                pe.wait_ge(att_ready, h + 1)
                dst = start(f"o{h}")
                for t in range(NT):
                    cols = slice(t * P, (t + 1) * P)
                    i = mm(dst[:, cols], v[:, t, h * DV:(h + 1) * DV], att[:, h, cols], start=True, stop=False,
                           skip_group_check=True)
                    parts = []
                    for cn in (2 * t, 2 * t + 1):
                        for s in range(2):
                            if cn >= SC and cn == (SC if s == 0 else NC - 1):
                                continue
                            first = cn == (0 if s == 0 else SC - 1)
                            parts.append((cn, s, sg0[rows_h, 2 * tt + s, :] if first else S[rows_h, 2 * tt + s, cn, :]))
                    for n, (cn, s, state) in enumerate(parts):
                        cc = slice(cn * CHUNK, (cn + 1) * CHUNK)
                        i = mm(dst[:, cc], state, qin[rows_h, 2 * tt + s, cc], start=False, stop=(n == len(parts) - 1),
                               skip_group_check=True)
                i.then_inc(product_ready, 1)
            wait_taken(pe, "o3")
            dst = start("ss")
            for h in range(HEADS):
                i = wide(dst[32 * h:32 * h + 32, :], ones[:, 0:32], sq[:, h, :], True, True)
            i.then_inc(product_ready, 1)
            pe.wait_ge(orms, 1)
            for h in range(HEADS):
                wide(start(f"rb{h}"), ones[32 * h:32 * h + 1, :], gd[32 * h:32 * h + 1, :], True, True).then_inc(product_ready, 1)

            def turn_rows(t):
                pe.wait_ge(h2_ready, t + 1)
                dst = start(f"hh{t}")
                for k in range(KD):
                    i = nc.tensor.transpose(dst[:, k * P:(k + 1) * P], h2[:, t % 2, k * P:(k + 1) * P], ident[:, :])
                i.then_inc(product_ready, 1)

            def router(t):
                wait_taken(pe, f"hh{t}")
                for k in range(KD):
                    i = mm(ms[:, 0, t * (NG + NE):(t + 1) * (NG + NE)], h2T[:, t % 2, k, :], rw[:, k, :],
                           start=(k == 0), stop=(k == KD - 1))
                i.then_inc(logits_ready, 1)

            pe.wait_ge(mix_ready, HEADS)
            wait_piece(pe, "wo0")
            wait_piece(pe, "wo1")
            pe.wait_ge(rows_t_out, 1)
            pe.wait_ge(lfin_t_out, 1)
            for t in range(NT):
                dst = start(f"mx{t}")
                for half in range(2):
                    w = weights(f"wo{half}")
                    for k in range(KD):
                        i = mm(dst[:, half * 512:(half + 1) * 512], mixT[:, k, t * P:(t + 1) * P], w[:, k, :],
                               start=(k == 0), stop=(k == KD - 1))
                i.then_inc(product_ready, 1)
                if t:
                    turn_rows(t - 1)
                if t >= 2:
                    router(t - 2)
            turn_rows(NT - 1)
            router(NT - 2)
            router(NT - 1)
            pe.wait_ge(choice, 1)
            pe.wait_ge(consts, 3)
            chosen = r16[:, 2, :, :]
            for t in range(NT):
                for t2 in range(t + 1):
                    mm(ms[:, 1, 128 + t * NE:128 + (t + 1) * NE], before[:, :] if t2 == t else ones[:, :], chosen[:, t2, :],
                       start=(t2 == 0), stop=(t2 == t))
            for t in range(NT):
                i = mm(ms[:, 1, 256:256 + NE], ones[:, :], chosen[:, t, :], start=(t == 0), stop=(t == NT - 1))
            i.then_inc(ranks, 1)
            for n in range(2 * NT):
                pe.wait_ge(onehots, n + 1)
                mm(ms[:, 0, 128:128 + 2 * NU], sel_a[:, n % 2, :], sel_b[:, n % 2, :], start=(n == 0), stop=(n == 2 * NT - 1)) \
                    .then_inc(onehots_used, 1)

            def turn_x(u):
                b = u % 2
                pe.wait_ge(gx_in[b], 16 * (u // 2 + 1))
                if u:
                    pe.wait_ge(x_taken, u)
                for k in range(KD):
                    i = nc.tensor.transpose(ps[:, 0, k * P:(k + 1) * P], gx[:, b, k * P:(k + 1) * P], ident[:, :])
                i.then_inc(x_turned, 1)

            def hidden(u):
                b = u % 2
                pe.wait_ge(x_taken, u + 1)
                pe.wait_ge(e13_in[u % 4], 16 * (u // 4 + 1))
                if u >= 2:
                    pe.wait_ge(act_ready, u - 1)
                for k in range(KD):
                    i = mm(ms[:, b, :], xgT[:, b, k, :], e13[u % 4][:, k, :], start=(k == 0), stop=(k == KD - 1))
                i.then_inc(hid, 1)

            def turn_a(u):
                b = u % 2
                pe.wait_ge(act_ready, u + 1)
                if u:
                    pe.wait_ge(a_taken, u)
                for k in range(DC):
                    i = nc.tensor.transpose(ps[:, 1, k * P:(k + 1) * P], act_sb[:, b, k * P:(k + 1) * P], ident[:, :])
                i.then_inc(a_turned, 1)

            def output(u):
                b = u % 2
                pe.wait_ge(a_taken, u + 1)
                pe.wait_ge(e2_in[u % 4], 16 * (u // 4 + 1))
                for half in range(2):
                    if u:
                        pe.wait_ge(y_taken, 2 * u - 1 + half)
                    for k in range(DC):
                        i = mm(ps[:, 2, half * 512:(half + 1) * 512], aT[:, b, k, :], e2[u % 4][:, k, half * 512:(half + 1) * 512],
                               start=(k == 0), stop=(k == DC - 1))
                    i.then_inc(y_done, 1)

            pe.wait_ge(routed, 1)
            turn_x(0)
            hidden(0)
            turn_x(1)
            hidden(1)
            for u in range(NE):
                turn_a(u)
                if u + 2 < NE:
                    turn_x(u + 2)
                output(u)
                if u + 2 < NE:
                    hidden(u + 2)
            pe.wait_ge(moe_done, 1)
            n_over = pe.value_load(eidi[0:1, NOV:NOV + 1], min_val=0, max_val=NOV)
            with pe.Fori(0, NOV) as i:
                with pe.If(n_over > i):
                    pe.wait_ge(ov["gx"], (i + 1) * 16)
                    for k in range(KD):
                        m = nc.tensor.transpose(ps[:, 0, k * P:(k + 1) * P], gx[:, 0, k * P:(k + 1) * P], ident[:, :])
                    m.then_inc(ov["xT"], 1)
                    pe.wait_ge(ov["w"], (i + 1) * 32)
                    pe.wait_ge(ov["xg"], i + 1)
                    for k in range(KD):
                        m = mm(ms[:, 0, :], xgT[:, 0, k, :], e13[0][:, k, :], start=(k == 0), stop=(k == KD - 1))
                    m.then_inc(ov["hid"], 1)
                    pe.wait_ge(ov["act"], i + 1)
                    for k in range(DC):
                        m = nc.tensor.transpose(ps[:, 1, k * P:(k + 1) * P], act_sb[:, 0, k * P:(k + 1) * P], ident[:, :])
                    m.then_inc(ov["aT"], 1)
                    pe.wait_ge(ov["at"], i + 1)
                    for half in range(2):
                        for k in range(DC):
                            m = mm(ps[:, 2, half * 512:(half + 1) * 512], aT[:, 0, k, :], e2[0][:, k, half * 512:(half + 1) * 512],
                                   start=(k == 0), stop=(k == DC - 1))
                    m.then_inc(ov["y"], 1)
                    pe.wait_ge(ov["out"], (i + 1) * 16)
                    pe.sem_inc(ov_turns, 1)
                pe.nop()

        @block.vector
        def _(dve):
            V = nc.vector
            tt_, ts_, stt = V.tensor_tensor, V.tensor_scalar, V.scalar_tensor_tensor
            n_chain = [0]

            def chain(ins):
                n_chain[0] += 1
                ins.then_inc(dve_chain, 1)

            def settle():
                dve.wait_ge(dve_chain, n_chain[0])

            def link(ins):
                chain(ins)
                settle()

            def ready(name):
                dve.wait_ge(product_ready, place[name] + 1)
                return product(name)

            dve.wait_ge(smt_ready, 1)
            chain(V.tensor_copy(adab[:, :], ms[:, 0, P:P + 6 * KD]))
            V.tensor_copy(smT[:, :], ms[:, 0, 0:NSM]).then_inc(smt_out, 1)
            dve.wait_ge(sums, 1)
            ts_(st[:, 1, :], st[:, 0, :], 1 / D, EPS, ALU.mult, ALU.add).then_inc(means, 1)
            dve.wait_ge(roots, 1)
            link(V.reciprocal(st[:, 0, :], st[:, 2, :]))
            for t in range(NT):
                i = ts_(xhat[:, t, :], xres[:, t, :], st[:, 0, t:t + 1], None, ALU.mult)
            i.then_inc(xhat_ready, 1)
            dve.wait_ge(smt_out, 1)
            dve.wait_ge(lam_exp, 1)
            link(ts_(lam[:, 2, :], lam[:, 1, :], 2.0, None, ALU.add))
            link(V.reciprocal(lam[:, 3, :], lam[:, 2, :]))
            link(tt_(lam[:, 2, :], lam[:, 1, :], lam[:, 3, :], ALU.mult))
            link(tt_(lam[:, 3, :], lam[:, 2, :], lam[:, 2, :], ALU.mult))
            link(ts_(lam[:, 4, :], lam[:, 3, :], 1 / 17, 1 / 15, ALU.mult, ALU.add))
            for n in (13, 11, 9, 7, 5, 3, 1):
                link(tt_(lam[:, 4, :], lam[:, 4, :], lam[:, 3, :], ALU.mult))
                link(ts_(lam[:, 4, :], lam[:, 4, :], 1 / n, None, ALU.add))
            link(tt_(lam[:, 4, :], lam[:, 4, :], lam[:, 2, :], ALU.mult))
            link(ts_(lam[:, 5, :], smT[:, LAM:LAM + 8], 0.0, None, ALU.min))
            link(stt(lam[:, 5, :], lam[:, 4, :], -2.0, lam[:, 5, :], ALU.mult, ALU.add))
            chain(ts_(lam[:, 3, :], lam[:, 5, :], RGLRU_C / 2, None, ALU.mult))
            ts_(lam[:, 4, :], lam[:, 5, :], -RGLRU_C / 4, None, ALU.mult).then_inc(lam_ready, 1)
            def take_mod(j):
                src = ready(f"aT{j}")[:, 0:512].rearrange("p (m r s) -> p m s r", m=4, r=4)[:, :, 0:2, :]
                V.tensor_reduce(mod[:, 4 * j:4 * j + 4, :], src, AX.X, ALU.add).then_inc(took["D"], 1)

            def add_bias(a, b):
                wait_taken(dve, f"aT{b // 4 - 1}")
                for s in range(2):
                    chain(tt_(mod[:, a:b, s], mod[:, a:b, s], adab[:, a:b], ALU.add))
                settle()

            for j in range(4):
                take_mod(j)
            add_bias(0, 2 * KD)
            for s in range(2):
                i = stt(A1[:, :, s], mod[:, KD:2 * KD, s], 1.0, smT[:, N1:N1 + KD], ALU.add, ALU.mult)
            i.then_inc(mod_out, 1)
            dve.wait_ge(mod_out, 1)
            for k in range(1, KD, 2):
                src = ready(f"xT{k}")
                ts_(hT[:, k, 0:NS], src[:, 0:NS], A1[:, k, 0:1], mod[:, k, 0:1], ALU.mult, ALU.add)
                ts_(hT[:, k, NS:N], src[:, NS:N], A1[:, k, 1:2], mod[:, k, 1:2], ALU.mult, ALU.add).then_inc(took["D"], 1)
            M = XLP - 3
            for ch in range(LC):
                wait_taken(dve, f"xl{ch}")
                settle()
                if ch:
                    dve.wait_ge(conv_ready, ch)

                def cw(j):
                    return smT[:, CW + 4 * j + ch:CW + 4 * j + ch + 1]
                link(ts_(cacc[:, 0:M], xlp[:, ch, 0:M], cw(0), smT[:, CB + ch:CB + ch + 1], ALU.mult, ALU.add))
                link(stt(cacc[:, 0:M], xlp[:, ch, 1:M + 1], cw(1), cacc[:, 0:M], ALU.mult, ALU.add))
                link(stt(cacc[:, 0:M], xlp[:, ch, 2:M + 2], cw(2), cacc[:, 0:M], ALU.mult, ALU.add))
                grid = (lambda ap, j: ap[:, j:j + PADS].rearrange("p (r w) -> p r w", w=PAD)[:, :, 0:GRID_W])
                chain(stt(xc[:, ch, 0:NS].rearrange("p (r w) -> p r w", w=GRID_W), grid(xlp[:, ch, :], 3), cw(3), grid(cacc, 0),
                          ALU.mult, ALU.add))
                stt(xc[:, ch, NS:N], xlp[:, ch, PADS + 3:XLP], cw(3), cacc[:, PADS:M], ALU.mult, ALU.add).then_inc(conv_ready, 1)
            dve.wait_ge(conv_ready, LC)
            take_mod(4)
            take_mod(5)
            for h in range(2):
                if h:
                    for j in range(6, 10):
                        take_mod(j)
                for ch in (2 * h, 2 * h + 1):
                    for s in range(2):
                        j = (ch % 2) * 2 + s
                        wait_taken(dve, f"lr{ch}{s}1")
                        chain(stt(ix[:, j, :], ix[:, j, :], 1.0, xc[:, ch, :], ALU.add, ALU.mult))
                for ch in (2 * h, 2 * h + 1):
                    for s in range(2):
                        j = (ch % 2) * 2 + s
                        dve.wait_ge(lru_sqrt, 4 * h + j + 1)
                        link(stt(tau[:, j, :], av[:, j, :], 1.0, tau[:, j, :], ALU.add, ALU.mult))
                        link(tt_(ix[:, j, :], ix[:, j, :], tau[:, j, :], ALU.mult))
                        rev = slice(None, None, -1) if s else slice(None)
                        hcol = smT[:, H0 + 4 * s + ch:H0 + 4 * s + ch + 1]
                        for part, init in ((slice(0, NS), hcol), (slice(NS, N), 0.0)):
                            xs = ix[:, j, part][:, rev]
                            chain(V.tensor_tensor_scan(tau[:, j, part][:, rev], av[:, j, part][:, rev], xs, init, ALU.mult, ALU.add))
                        settle()
                        end = N - 1 if s == 0 else NS
                        V.tensor_copy(lfin[:, 4 * s + ch:4 * s + ch + 1], tau[:, j, end:end + 1]).then_inc(lfin_ready, 1)
                    j = (ch % 2) * 2
                    link(tt_(tau[:, j, :], tau[:, j, :], tau[:, j + 1, :], ALU.add))
                    wait_taken(dve, f"yl{ch}")
                    i = tt_(mixT[:, ch, :], mixT[:, ch, :], tau[:, j, :], ALU.mult)
                    if ch % 2 == 0:
                        chain(i)
                i.then_inc(lru_done, 1)
            dve.wait_ge(lru_done, 2)
            take_mod(10)
            take_mod(11)
            for g in range(4):
                dve.wait_ge(zlog, g + 1)
                link(stt(bcum[:, g, :], bcum[:, g, :], 0.0, gt[:, g, :], ALU.min, ALU.subtract))
                if g == 0:
                    dve.wait_ge(scan_mask, 1)
                rev = slice(None, None, -1) if g % 2 else slice(None)
                V.tensor_tensor_scan(bcum[:, g, :][:, rev], gd[:, :], bcum[:, g, :][:, rev], 0.0, ALU.mult, ALU.add).then_inc(bready, 1)

            def modulation():
                add_bias(2 * KD, 6 * KD)
                for s in range(2):
                    chain(V.tensor_copy(A2[:, 4 * s + 0, :], mod[:, 2 * KD:3 * KD, s]))
                    chain(stt(A2[:, 4 * s + 1, :], mod[:, 4 * KD:5 * KD, s], 1.0, smT[:, N2:N2 + KD], ALU.add, ALU.mult))
                    chain(V.tensor_copy(A2[:, 4 * s + 2, :], mod[:, 3 * KD:4 * KD, s]))
                    i = V.tensor_copy(A2[:, 4 * s + 3, :], mod[:, 5 * KD:6 * KD, s])
                    if s == 0:
                        chain(i)
                i.then_inc(mod_out, 1)

            def chunks(ap):
                return ap.rearrange("p (c i) -> p c i", i=CHUNK)

            def differences(g):
                r = 3 * (g % 2)
                s = g % 2
                mid, last = (CHUNK // 2 - 1, CHUNK - 1) if s == 0 else (CHUNK // 2, 0)
                b = chunks(bcum[:, g, :])
                dve.wait_ge(bready, 4)
                if g >= 2:
                    wait_taken(dve, f"at{g - 2}1")
                    wait_taken(dve, f"kT{g - 2}")
                chain(tt_(chunks(gt[:, r, :]), b, b[:, :, mid:mid + 1].to_broadcast([P, NC, CHUNK]), ALU.subtract))
                tt_(chunks(gt[:, r + 2, :]), b[:, :, last:last + 1].to_broadcast([P, NC, CHUNK]), b, ALU.subtract).then_inc(diffs, 1)

            def scale_qk(g):
                r = 3 * (g % 2)
                dve.wait_ge(exps, g + 1)
                tt_(gt[:, r, :], gt[:, r, :], q[:, g // 2, :], ALU.mult)
                tt_(gt[:, r + 1, :], gt[:, r + 1, :], kk[:, g // 2, :], ALU.mult).then_inc(qk_ready, 1)

            def scores(g):
                s = g % 2
                m = mask[:, s:s + 1, :].bitcast(U32).to_broadcast([P, NT, P])
                for hh in range(2):
                    h = 2 * (g // 2) + hh
                    src = ready(f"at{g}{hh}")[:, 0:N].rearrange("p (t i) -> p t i", i=P)
                    dst = att[:, h, :] if s == 0 else attb[:, :]
                    if s and h:
                        dve.wait_ge(att_ready, h)
                    V.copy_predicated(dst.rearrange("p (t i) -> p t i", i=P), m, src).then_inc(took["D"], 1)
                    if s:
                        wait_taken(dve, f"at{g}{hh}")
                        tt_(att[:, h, :], att[:, h, :], attb[:, :], ALU.add).then_inc(att_ready, 1)

            def carry(g):
                s = g % 2
                src = ready(f"kvA{g}")

                def kv(cn, base, first):
                    col = (cn % 2) * 512 + (cn - first) // 2 * DV
                    return base[:, col:col + DV]
                seq = list(range(SC)) if s == 0 else list(range(SC - 1, -1, -1))
                state = sg0[:, g, :]
                dve.wait_ge(qin_ready, g + 1)
                for a, b in zip(seq[:-1], seq[1:]):
                    i = stt(S[:, g, b, :], state, dec[:, g, a:a + 1], kv(a, src, 0), ALU.mult, ALU.add)
                    if b != seq[-1]:
                        link(i)
                    state = S[:, g, b, :]
                i.then_inc(took["D"], 1)
                src = ready(f"kvB{g}")
                a, b = (SC, SC + 1) if s == 0 else (SC + 1, SC)
                link(V.tensor_copy(S[:, g, b, :], kv(a, src, SC)))
                stt(sfin[:, g, :], S[:, g, b, :], dec[:, g, b:b + 1], kv(b, src, SC), ALU.mult, ALU.add).then_inc(took["D"], 1)

            differences(0)
            differences(1)
            modulation()
            dve.wait_ge(att_zero, 1)
            dve.wait_ge(consts, 3)
            dve.wait_ge(sg_in, 16 * 4)
            for g in range(4):
                scale_qk(g)
                if g == 0:
                    dve.wait_ge(rowsT, 1)
                    dve.wait_ge(lfinT, 1)
                    V.tensor_copy(rows_t[:, :], ms[0:8 * KD, 0, 0:P]).then_inc(rows_t_out, 1)
                    V.tensor_copy(lfin_t[:, :], ms[0:8, 0, P:2 * P]).then_inc(lfin_t_out, 1)
                scores(g)
                carry(g)
                if g + 2 < 4:
                    differences(g + 2)
            dve.wait_ge(took["A"], count("ss")[1])
            V.reciprocal(gd[:, :], gd[:, :]).then_inc(orms, 1)
            for h in range(HEADS):
                stt(osb[:, h, :], osb[:, h, :], smT[:, GN:GN + 1], ready(f"rb{h}")[:, 0:N], ALU.mult, ALU.mult).then_inc(took["D"], 1)
                wait_taken(dve, f"rb{h}")
                i = tt_(mixT[:, LC + h, :], mixT[:, LC + h, :], osb[:, h, :], ALU.mult)
                i.then_inc(mix_ready, 1)
            for t in range(NT):
                seq = 0 if t < ST else 1
                dve.wait_ge(rows_in[seq], 16 * 4)
                if t:
                    dve.wait_ge(sums, 1 + t)
                stt(mtmp, ready(f"mx{t}"), 1.0, rows[seq][0], ALU.mult, ALU.mult).then_inc(took["D"], 1)
                wait_taken(dve, f"mx{t}")
                tt_(xres[:, t, :], xres[:, t, :], mtmp, ALU.add).then_inc(rd_ready, 1)
                dve.wait_ge(sums, 2 + t)
                ts_(rt[:, 0, t:t + 1], st[:, 3, t:t + 1], 1 / D, EPS, ALU.mult, ALU.add).then_inc(means, 1)
                dve.wait_ge(roots, 2 + t)
                link(V.reciprocal(rt[:, 2, t:t + 1], rt[:, 1, t:t + 1]))
                if t >= 2:
                    dve.wait_ge(h2_out[t % 2], 16 * (t // 2))
                    wait_taken(dve, f"hh{t - 2}")
                link(stt(h2[:, t % 2, :], xres[:, t, :], rt[:, 2, t:t + 1], rows[seq][1], ALU.mult, ALU.mult))
                tt_(h2[:, t % 2, :], h2[:, t % 2, :], rows[seq][2], ALU.add).then_inc(h2_ready, 1)
            dve.wait_ge(logits_ready, NT)
            lgv = ms[:, 0, 0:NT * (NG + NE)].rearrange("p (t e) -> p t e", t=NT)
            b20 = rbias[:, :].rearrange("p (a e) -> p a e", a=1).to_broadcast([P, NT, NG + NE])
            link(tt_(lg[:, :, :], lgv, b20, ALU.add))

            def bc(ap, n):
                return ap.rearrange("p (t a) -> p t a", a=1).to_broadcast([P, NT, n])

            w4b = w4[:, :].rearrange("p (a e) -> p a e", a=1).to_broadcast([P, NT, NG])

            def first_max(dst, src, mx, scratch):
                link(V.tensor_reduce(mx, src, AX.X, ALU.max))
                link(tt_(scratch, src, bc(mx, NG), ALU.is_equal))
                link(tt_(scratch, scratch, w4b, ALU.mult))
                link(V.tensor_reduce(rt[:, 7, :], scratch, AX.X, ALU.max))
                link(tt_(dst, scratch, bc(rt[:, 7, :], NG), ALU.is_equal))

            first_max(r4[:, 2, :, :], lg[:, :, 0:NG], rt[:, 3, :], r4[:, 1, :, :])
            tt_(r4[:, 0, :, :], lg[:, :, 0:NG], bc(rt[:, 3, :], NG), ALU.subtract).then_inc(gready, 1)
            le = lg[:, :, NG:]

            def outer(dst, e4):
                for gi in range(NG):
                    chain(tt_(dst[:, :, gi * EG:(gi + 1) * EG], e4, r4[:, 2, :, gi:gi + 1].to_broadcast([P, NT, EG]), ALU.mult))
                settle()

            for gi in range(NG):
                chain(tt_(r16[:, 0, :, gi * EG:(gi + 1) * EG], le[:, :, gi * EG:(gi + 1) * EG],
                          r4[:, 2, :, gi:gi + 1].to_broadcast([P, NT, EG]), ALU.mult))
            settle()
            a0 = r16[:, 0, :, :]
            chain(tt_(r4[:, 5, :, :], a0[:, :, 0:EG], a0[:, :, EG:2 * EG], ALU.add))
            chain(tt_(r4[:, 6, :, :], a0[:, :, 2 * EG:3 * EG], a0[:, :, 3 * EG:4 * EG], ALU.add))
            settle()
            link(tt_(r4[:, 5, :, :], r4[:, 5, :, :], r4[:, 6, :, :], ALU.add))
            link(V.tensor_reduce(rt[:, 4, :], r4[:, 5, :, :], AX.X, ALU.max))
            tt_(r4[:, 3, :, :], r4[:, 5, :, :], bc(rt[:, 4, :], EG), ALU.subtract).then_inc(eready, 1)
            dve.wait_ge(gexp, 1)
            link(V.tensor_reduce(rt[:, 5, :], r4[:, 1, :, :], AX.X, ALU.add))
            link(V.reciprocal(rt[:, 5, :], rt[:, 5, :]))
            dve.wait_ge(eexp, 1)
            ex = r4[:, 4, :, :]
            first_max(r4[:, 5, :, :], ex, rt[:, 0, :], r4[:, 7, :, :])
            link(stt(ex, r4[:, 5, :, :], -2.0, ex, ALU.mult, ALU.add))
            first_max(r4[:, 6, :, :], ex, rt[:, 1, :], r4[:, 7, :, :])
            link(tt_(rt[:, 2, :], rt[:, 0, :], rt[:, 1, :], ALU.add))
            link(V.reciprocal(rt[:, 2, :], rt[:, 2, :]))
            link(tt_(rt[:, 2, :], rt[:, 2, :], rt[:, 5, :], ALU.mult))
            for i2 in range(2):
                chain(tt_(rt[:, i2, :], rt[:, i2, :], rt[:, 2, :], ALU.mult))
            outer(r16[:, 0, :, :], r4[:, 5, :, :])
            outer(r16[:, 1, :, :], r4[:, 6, :, :])
            tt_(r16[:, 2, :, :], r16[:, 0, :, :], r16[:, 1, :, :], ALU.add).then_inc(choice, 1)
            dve.wait_ge(ranks, 1)
            link(V.tensor_copy(cnt[:, 0, :], ms[:, 1, 256:256 + NE]))
            link(ts_(cnt[:, 1, :], cnt[:, 0, :], float(P), None, ALU.is_gt))
            for m in range(2, NT):
                link(stt(cnt[:, 1, :], cnt[:, 0, :], float(m * P), cnt[:, 1, :], ALU.is_gt, ALU.add))
            link(ts_(cnt[:, 4, :], cnt[:, 1, :], 0.0, 1.0, ALU.mult, ALU.add))
            link(V.tensor_tensor_scan(cnt[:, 2, :], cnt[:, 4, :], cnt[:, 1, :], 0.0, ALU.mult, ALU.add))
            link(tt_(cnt[:, 3, :], cnt[:, 2, :], cnt[:, 1, :], ALU.subtract))
            link(ts_(cnt[:, 3, :], cnt[:, 3, :], float(NE - 1), None, ALU.add))
            for i2 in range(NOV):
                chain(ts_(eid_c[:, i2, :], cnt[:, 2, :], float(i2), None, ALU.is_le))
            settle()
            link(V.tensor_reduce(eidf[:, 0:NOV], eid_c[:, :, :], AX.X, ALU.add))
            link(ts_(eidf[:, 0:NOV], eidf[:, 0:NOV], float(NE - 1), None, ALU.min))
            chain(V.tensor_copy(eidf[:, NOV:NOV + 1], cnt[:, 2, NE - 1:NE]))
            settle()
            chain(V.tensor_copy(eidi[:, :], eidf[:, :]))
            rk = ms[:, 1, 128:128 + NT * NE].rearrange("p (t e) -> p t e", t=NT)

            def across(row):
                return row.rearrange("p (a e) -> p a e", a=1).to_broadcast([P, NT, NE])

            for i2 in range(2):
                oh = r16[:, i2, :, :]
                for n, (what, dst) in enumerate(((rk, rt[:, 3, :]), (across(io16[:, :]), rt[:, 4, :]), (across(cnt[:, 3, :]), rt[:, 5, :]))):
                    link(tt_(r16[:, 3, :, :], oh, what, ALU.mult))
                    link(V.tensor_reduce(dst, r16[:, 3, :, :], AX.X, ALU.add))
                link(ts_(rt[:, 6, :], rt[:, 3, :], float(P), None, ALU.is_ge))
                for m in range(2, NT):
                    link(stt(rt[:, 6, :], rt[:, 3, :], float(m * P), rt[:, 6, :], ALU.is_ge, ALU.add))
                link(stt(rt[:, 3, :], rt[:, 6, :], -float(P), rt[:, 3, :], ALU.mult, ALU.add))
                link(ts_(rt[:, 7, :], rt[:, 6, :], 1.0, None, ALU.min))
                link(tt_(rt[:, 5, :], rt[:, 5, :], rt[:, 6, :], ALU.add))
                link(tt_(rt[:, 5, :], rt[:, 5, :], rt[:, 4, :], ALU.subtract))
                link(tt_(rt[:, 5, :], rt[:, 5, :], rt[:, 7, :], ALU.mult))
                link(tt_(rt[:, 4, :], rt[:, 4, :], rt[:, 5, :], ALU.add))
                link(stt(rt[:, 5, :], rt[:, 4, :], float(P), rt[:, 3, :], ALU.mult, ALU.add))
                chain(V.tensor_copy(yidx[:, i2 * NT:(i2 + 1) * NT], rt[:, 5, :]))
                for t in range(NT):
                    n = i2 * NT + t
                    b = n % 2
                    if n >= 2:
                        dve.wait_ge(onehots_used, n - 1)
                    chain(ts_(sel_a[:, b, :], io128[:, :], rt[:, 3, t:t + 1], None, ALU.is_equal))
                    chain(ts_(sel_b[:, b, 0:NU], iou[:, :], rt[:, 4, t:t + 1], tokid[:, t:t + 1], ALU.is_equal, ALU.mult))
                    settle()
                    ts_(sel_b[:, b, NU:2 * NU], iou[:, :], rt[:, 4, t:t + 1], rt[:, i2, t:t + 1], ALU.is_equal, ALU.mult) \
                        .then_inc(onehots, 1)
            dve.wait_ge(onehots_used, 2 * NT)
            chain(ts_(slot_tok[:, :], ms[:, 0, 128:128 + NU], float(N), None, ALU.add))
            settle()
            V.tensor_copy(slot_gate[:, :], ms[:, 0, 128 + NU:128 + 2 * NU]).then_inc(routed, 1)
            dve.wait_ge(routed, 1)

            def take_x(u):
                dve.wait_ge(x_turned, u + 1)
                if u >= 2:
                    dve.wait_ge(hid, u - 1)
                V.tensor_copy(xgT[:, u % 2, :, :].rearrange("p k n -> p (k n)"), ps[:, 0, :]).then_inc(x_taken, 1)

            def activate(u):
                b = u % 2
                dve.wait_ge(silu, u + 1)
                if u >= 2:
                    dve.wait_ge(a_turned, u - 1)
                stt(act_sb[:, b, :], sact[:, b, :], slot_gate[:, u:u + 1], ms[:, b, DE:2 * DE], ALU.mult, ALU.mult).then_inc(act_ready, 1)

            def take_a(u):
                b = u % 2
                dve.wait_ge(a_turned, u + 1)
                if u >= 2:
                    dve.wait_ge(y_done, 2 * (u - 1))
                V.tensor_copy(aT[:, b, :, :].rearrange("p k n -> p (k n)"), ps[:, 1, 0:DE]).then_inc(a_taken, 1)

            take_x(0)
            take_x(1)
            activate(0)
            activate(1)
            for u in range(NE):
                take_a(u)
                if u + 2 < NE:
                    take_x(u + 2)
                    activate(u + 2)
            dve.wait_ge(moe_done, 1)
            n_over = dve.value_load(eidi[0:1, NOV:NOV + 1], min_val=0, max_val=NOV)
            with dve.Fori(0, NOV) as i:
                with dve.If(n_over > i):
                    V.tensor_copy(ov_gate[:, :], slot_gate[:, bass.ds(i + NE, 1)])
                    V.tensor_copy(ov_tok[:, :], slot_tok[:, bass.ds(i + NE, 1)]).then_inc(ov["tok"], 1)
                    dve.wait_ge(ov["tok"], i + 1)
                    dve.wait_ge(ov["xT"], i + 1)
                    V.tensor_copy(xgT[:, 0, :, :].rearrange("p k n -> p (k n)"), ps[:, 0, :]).then_inc(ov["xg"], 1)
                    dve.wait_ge(ov["silu"], i + 1)
                    stt(act_sb[:, 0, :], sact[:, 0, :], ov_gate[:, :], ms[:, 0, DE:2 * DE], ALU.mult, ALU.mult).then_inc(ov["act"], 1)
                    dve.wait_ge(ov["aT"], i + 1)
                    V.tensor_copy(aT[:, 0, :, :].rearrange("p k n -> p (k n)"), ps[:, 1, 0:DE]).then_inc(ov["at"], 1)
                    dve.wait_ge(ov["out"], (i + 1) * 16)
                    dve.sem_inc(ov_turns, 1)
                dve.nop()
            dve.wait_ge(fg_in, 16)
            for t in range(NT):
                seq = 0 if t < ST else 1
                b = t % 2
                dve.wait_ge(yg_in[b], 32 * (t // 2 + 1))
                y1, y2 = yg[:, 2 * b, :], yg[:, 2 * b + 1, :]
                link(tt_(y1, y1, y2, ALU.add))
                link(tt_(y1, y1, rows[seq][3], ALU.mult))
                tt_(xres[:, t, :], xres[:, t, :], y1, ALU.add).then_inc(rd_ready, 1)
                dve.wait_ge(sums, 2 + NT + t)
                ts_(st[:, 1, t:t + 1], st[:, 0, t:t + 1], 1 / D, EPS, ALU.mult, ALU.add).then_inc(means, 1)
                dve.wait_ge(roots, 2 + NT + t)
                V.reciprocal(st[:, 3, t:t + 1], st[:, 2, t:t + 1]).then_inc(yg_used, 1)
                dve.wait_ge(yg_used, t + 1)
                stt(xres[:, t, :], xres[:, t, :], st[:, 3, t:t + 1], fing, ALU.mult, ALU.mult).then_inc(ready_out, 1)


_INS = ['x_prompt', 'x_sample', 'state_lru', 'state_gla', 'c', 'c_ctx', 'ada_w', 'ada_b', 'norm1_g', 'w_in',
        'conv_w', 'conv_b', 'lru_wr', 'lru_br', 'lru_wi', 'lru_bi', 'lru_lam', 'gla_wg', 'gla_bg',
        'gla_norm_g', 'w_out', 'norm2_g', 'router_gw', 'router_gb', 'router_ew', 'router_eb', 'exp_w13',
        'exp_w2', 'final_g']
_OUTS = ['x_prompt', 'x_sample', 'state_lru', 'state_gla']


def kernel(**inputs):
    import numpy as _np
    import concourse.bacc as _bacc
    from concourse import mybir as _mybir
    from concourse.bass_utils import run_bass_kernel_spmd as _run

    nc = _bacc.Bacc("TRN2", target_bir_lowering=False, num_devices=1)
    arrays, args = {}, []
    for name in _INS:
        a = _np.ascontiguousarray(inputs[name])
        arrays[f"in_{name}_dram"] = a
        args.append(nc.dram_tensor(f"in_{name}_dram", a.shape, _mybir.dt.from_np(a.dtype), kind="ExternalInput").ap())
    for i, like in enumerate(_OUTS):
        a = inputs[like]
        args.append(nc.dram_tensor(f"out_{i}_dram", a.shape, _mybir.dt.from_np(_np.dtype(a.dtype)), kind="ExternalOutput").ap())
    hybrid_step(nc, *args)
    r = _run(nc, [arrays], core_ids=[0])
    return tuple(r.results[0][f"out_{i}_dram"] for i in range(len(_OUTS)))
```

```python
from contextlib import ExitStack

import concourse.bass as bass
from concourse import mybir

F32 = mybir.dt.float32
I32 = mybir.dt.int32
U32 = mybir.dt.uint32
ALU = mybir.AluOpType
ACT = mybir.ActivationFunctionType
AX = mybir.AxisListType

P = 128
EPS = 1e-6
GRID_W = 64
CHUNK = 64
RGLRU_C = 8.0
GLA_TAU = 16.0


def hybrid_step(nc, x_prompt, x_sample, state_lru, state_gla, c, c_ctx, ada_w, ada_b, norm1_g, w_in,
                conv_w, conv_b, lru_wr, lru_br, lru_wi, lru_bi, lru_lam, gla_wg, gla_bg, gla_norm_g,
                w_out, norm2_g, router_gw, router_gb, router_ew, router_eb, exp_w13, exp_w2, final_g,
                y_prompt, y_sample, state_lru_new, state_gla_new):
    D = x_sample.shape[2]
    NS = x_sample.shape[1]
    NP = x_prompt.shape[1]
    N = NS + NP
    KD = D // P
    NT = N // P
    ST = NS // P
    LW = lru_br.shape[2]
    LC = LW // P
    LB = lru_wr.shape[3]
    HEADS, DK, DV = state_gla.shape[3:]
    QK = HEADS * DK
    QT = QK // P
    RANK = gla_wg.shape[2]
    NC = N // CHUNK
    SC = NS // CHUNK
    NG = router_gw.shape[2]
    NE = router_ew.shape[2]
    EG = NE // NG
    DE = exp_w2.shape[2]
    DC = DE // P
    NOV = 2 * N // P - 1
    NU = NE + NOV
    PAD = GRID_W + 3
    PADS = NS // GRID_W * PAD
    XLP = PADS + NP + 3
    assert (D, N, LC, QT, DV, NE, DC, NT) == (1024, 640, 4, 2, P, 16, 2, 5)

    x_s = x_sample[0]
    x_p = x_prompt[0]

    rows_d = nc.dram_tensor("mod_rows", [8 * D], F32).ap()
    h2_d = nc.dram_tensor("h2_rows", [N + 1, D], F32).ap()
    y_d = nc.dram_tensor("expert_rows", [NU * P, D], F32).ap()

    ctx = ExitStack()
    with ctx:
        def sb(name, shape, dt=F32):
            return ctx.enter_context(nc.sbuf_tensor(name, shape, dt))

        def sem(name):
            return ctx.enter_context(nc.semaphore(name))

        W_WORDS = KD * 512
        wring = sb("wring", [P, 3, W_WORDS])
        xres = sb("xres", [P, NT, D])
        mixT = sb("mixT", [P, KD, N])
        r1 = sb("r1", [P, KD * N])
        vtok = sb("vtok", [P, NT * 512])
        qk = sb("qk", [P, 4 * N])
        gd = sb("gd", [P, N])
        TMPW = 12 * N + LC * XLP + LC * N + XLP + 16 * P
        tmp = sb("tmp", [P, TMPW])
        hT = r1[:, :].rearrange("p (k n) -> p k n", k=KD)
        S = r1[:, :].rearrange("p (g c v) -> p g c v", g=4, c=NC)
        v = vtok[:, :].rearrange("p (t n) -> p t n", t=NT)
        q = qk[:, 0:2 * N].rearrange("p (t n) -> p t n", t=2)
        kk = qk[:, 2 * N:4 * N].rearrange("p (t n) -> p t n", t=2)
        xhat = tmp[:, 0:NT * D].rearrange("p (t d) -> p t d", t=NT)
        tau = tmp[:, 0:4 * N].rearrange("p (j n) -> p j n", j=4)
        av = tmp[:, 4 * N:8 * N].rearrange("p (j n) -> p j n", j=4)
        ix = tmp[:, 8 * N:12 * N].rearrange("p (j n) -> p j n", j=4)
        o0 = 12 * N
        xlp = tmp[:, o0:o0 + LC * XLP].rearrange("p (c n) -> p c n", c=LC)
        o0 += LC * XLP
        xc = tmp[:, o0:o0 + LC * N].rearrange("p (c n) -> p c n", c=LC)
        o0 += LC * N
        cacc = tmp[:, o0:o0 + XLP]
        o0 += XLP
        lruw = tmp[:, o0:o0 + 16 * P].rearrange("p (w s c n) -> p w s c n", w=2, s=2, c=LC)
        bcum = tmp[:, 0:4 * N].rearrange("p (g n) -> p g n", g=4)
        gt = tmp[:, 4 * N:10 * N].rearrange("p (j n) -> p j n", j=6)
        kdT = tmp[:, 10 * N:14 * N].rearrange("p (g n) -> p g n", g=4)
        qin = tmp[:, 14 * N:18 * N].rearrange("p (g n) -> p g n", g=4)
        att = tmp[:, 18 * N:22 * N].rearrange("p (h n) -> p h n", h=HEADS)
        attb = tmp[:, 22 * N:23 * N]
        otok = tmp[:, 10 * N:10 * N + 1024].rearrange("p (b n) -> p b n", b=2)
        osq = tmp[:, 10 * N + 1024:10 * N + 1024 + 4 * DV]
        orms = tmp[:, 23 * N:23 * N + 3 * 4 * NT].rearrange("p (a t h) -> p a t h", a=3, t=NT)
        rows = [[tmp[:, 0:D], tmp[:, D:2 * D], tmp[:, 4 * N:4 * N + D], tmp[:, 4 * N + D:4 * N + 2 * D]],
                [tmp[:, 10 * N:10 * N + D], tmp[:, 10 * N + D:10 * N + 2 * D], qk[:, 0:D], qk[:, D:2 * D]]]
        o0 = 14 * N
        h2 = tmp[:, o0:o0 + 2 * D].rearrange("p (b d) -> p b d", b=2)
        h2T = tmp[:, o0 + 2 * D:o0 + 4 * D].rearrange("p (b k n) -> p b k n", b=2, k=KD)
        mtmp = tmp[:, o0 + 4 * D:o0 + 5 * D]
        e13 = [r1[:, 0:W_WORDS], wring[:, 1, :], wring[:, 2, :], tmp[:, o0:o0 + W_WORDS]]
        e13 = [w.rearrange("p (k f) -> p k f", k=KD) for w in e13]
        mix_flat = mixT[:, :, :].rearrange("p k n -> p (k n)")
        e2 = [vtok[:, 0:DC * D], wring[:, 0, 0:DC * D], wring[:, 0, DC * D:2 * DC * D], mix_flat[:, 0:DC * D]]
        e2 = [w.rearrange("p (k f) -> p k f", k=DC) for w in e2]
        junk = r1[:, :].rearrange("p (t d) -> p t d", t=NT)
        gx = mix_flat[:, DC * D:DC * D + 2 * D].rearrange("p (b d) -> p b d", b=2)
        xgT = tmp[:, 0:2 * D].rearrange("p (b k n) -> p b k n", b=2, k=KD)
        ysb = tmp[:, 10 * N:10 * N + 2 * D].rearrange("p (b d) -> p b d", b=2)
        sact = tmp[:, 10 * N + 2 * D:10 * N + 2 * D + 2 * DE].rearrange("p (b f) -> p b f", b=2)
        act_sb = vtok[:, DC * D:DC * D + 2 * DE].rearrange("p (b f) -> p b f", b=2)
        aT = gd[:, 0:2 * DE].rearrange("p (b k n) -> p b k n", b=2, k=DC)
        wring_flat = wring[:, :, :].rearrange("p s n -> p (s n)")
        yg = wring_flat[:, 0:2 * NT * D].rearrange("p (b d) -> p b d", b=2 * NT)
        fing = wring_flat[:, 2 * NT * D:(2 * NT + 1) * D]

        PE_SUMS = (3, 4)
        NSM = 89
        sm_in = mix_flat[:, D:D + P]
        adab_in = mix_flat[0:6 * KD, D + P:D + 2 * P]
        smT = sb("smT", [P, NSM])
        adab = sb("adab", [P, 6 * KD])
        cs = sb("cs", [P, KD, 32])
        mod = sb("mod", [P, 6 * KD, 2])
        A1 = sb("A1", [P, KD, 2])
        A2 = sb("A2", [P, 8, KD])
        rows_t = sb("rows_t", [8 * KD, P])
        sg0 = sb("sg0", [P, 4, DV])
        sfin = sb("sfin", [P, 4, DV])
        adrow = [s[:, :, :].rearrange("p g v -> p (g v)") for s in (sg0, sfin)]
        eps = sb("eps", [P, 1])
        zero = sb("zero", [P, P])
        ident = sb("ident", [P, P])
        ones = sb("ones", [P, P])
        before = sb("before", [P, P])
        mask = sb("mask", [P, 2, P])
        wgb = sb("wgb", [2 * RANK, 2 * QK])
        wgd = sb("wgd", [P, KD, 2 * RANK])
        hb = sb("hb", [P, 16])
        lam = sb("lam", [P, 6, 8])
        lfin = sb("lfin", [P, 8])
        lfin_t = sb("lfin_t", [8, P])
        dec = sb("dec", [P, 4, NC])
        st = sb("st", [P, 4, NT])
        rw = sb("rw", [P, KD, NG + NE])
        rbias = sb("rbias", [P, NG + NE])
        free = [0]

        def scratch_of(a, b):
            w = tmp[:, free[0]:free[0] + a * b]
            free[0] += a * b
            assert free[0] <= 4 * N + D
            return w.rearrange("p (a b) -> p a b", a=a)

        lg = scratch_of(NT, NG + NE)
        r4 = scratch_of(8, NT * NG).rearrange("p a (t e) -> p a t e", t=NT)
        r16 = scratch_of(4, NT * NE).rearrange("p a (t e) -> p a t e", t=NT)
        sel_a = scratch_of(2 * NT, P)
        sel_b = scratch_of(2 * NT, 2 * NU)
        oh_scr = scratch_of(2, NT * NE).rearrange("p a (t e) -> p a t e", t=NT)
        th_scr = scratch_of(NE, NT - 1)
        rt2 = scratch_of(6, 2 * NT)
        eid_c = scratch_of(NOV, NE)
        rt = sb("rt", [P, 8, NT])
        w4 = sb("w4", [P, NG])
        numbers = sb("numbers", [P, P])
        tokid = sb("tokid", [P, NT])
        thresholds = sb("thresholds", [P, NT - 1])
        cnt = sb("cnt", [P, 6, NE])
        eidf = sb("eidf", [P, NOV + 1])
        eidi = sb("eidi", [P, NOV + 1], I32)
        slot_tok = sb("slot_tok", [P, NU], I32)
        slot_gate = sb("slot_gate", [P, NU])
        yidx = sb("yidx", [P, 2 * NT], I32)
        ov_tok = sb("ov_tok", [P, 1], I32)
        ov_gate = sb("ov_gate", [P, 1])

        ps = ctx.enter_context(nc.psum_tensor("ps", [P, 3, 1024], F32))
        ms = ctx.enter_context(nc.psum_tensor("ms", [P, 2, 512], F32))

        order = []
        for j in range(4):
            order += [(f"ad{j}", "A")] + [(f"aT{j - 1}", "D")] * (j > 0)
        order += [("aT3", "D")]
        order += [(f"xT{k}", "AD"[k % 2]) for k in range(KD)]

        def modulation_order(j, between):
            return [(f"ad{j}", "A"), (f"ad{j + 1}", "A")] + between + [(f"aT{j}", "D"), (f"aT{j + 1}", "D")]

        def gates_order(ch, s):
            return [(f"lr{ch}{s}{w}", "A") for w in range(2)]

        order += [(f"xl{t}", "A") for t in range(LC)]
        for n in range(4):
            step = gates_order(n // 2, n % 2) + [(f"yl{n}", "A")]
            order += step if n else modulation_order(4, step)
        order += modulation_order(6, [])
        order += [(f"k{t}", "A") for t in range(QT)] + [(f"q{t}", "A") for t in range(QT)] + [("gd", "A")]
        for n in range(4):
            step = gates_order(2 + n // 2, n % 2) + [(f"v{n}", "A")]
            order += step if n else modulation_order(8, step)
        order += [("v4", "A")] + modulation_order(10, [("og0", "A")])
        order += [(f"g{g}", "A") for g in range(4)] + [("og1", "A")]
        for g in range(4):
            order += [("og2", "A")] * (g == 0) + [(f"kT{g}", "A"), (f"at{g}0", "D"), (f"at{g}1", "D")]
            order += [("og3", "A")] * (g == 0) + [(f"kvA{g}", "D"), (f"kvB{g}", "D")]
        for t in range(NT):
            order += [(f"o{t}", "D")] + [(f"oT{t - 1}", "D")] * (t > 0)
        for t in range(NT):
            order += [(f"mx{t}", "D")] + [(f"oT{NT - 1}", "D")] * (t == 0)
            if t:
                order += [(f"hh{t - 1}", "A")]
        order += [(f"hh{NT - 1}", "A")]
        place = {name: n for n, (name, _) in enumerate(order)}
        RING = 3

        def product(name):
            return ps[:, place[name] % RING, :]

        wi = w_in[0].rearrange("(k p) n -> p k n", p=P)
        aw = ada_w[0].rearrange("(k p) n -> p k n", p=P)
        wo = w_out[0].rearrange("(k p) n -> p k n", p=P)
        QK0, V0, OG0, GD0 = 2 * LW, 2 * LW + 2 * QK, 2 * LW + 2 * QK + HEADS * DV, 2 * LW + 2 * QK + 2 * HEADS * DV
        pieces = [(f"a{j}", aw[:, :, 512 * j:512 * j + 512]) for j in range(4)]
        for n, (name, col) in enumerate((("xl", 0), ("yl", LW), ("qk", QK0), ("v", V0), ("og", OG0))):
            pieces += [(name, wi[:, :, col:col + 512])]
            if n < 4:
                pieces += [(f"a{j}", aw[:, :, 512 * j:512 * j + 512]) for j in (2 * n + 4, 2 * n + 5)]
        pieces += [(f"wo{j}", wo[:, :, 512 * j:512 * j + 512]) for j in range(2)]
        piece = {name: n for n, (name, _) in enumerate(pieces)}

        tiled = {"yl": ([f"xl{i}" for i in range(4)], 0), "qk": ([f"yl{i}" for i in range(4)], 1), "og": (["v4"] * 4, 2)}
        last_use = {"qk": "q1", "xl": "xl3", "yl": "yl3", "v": "v4", "og": "og3"}

        def weights(name):
            return wring[:, piece[name] % 3, :].rearrange("p (k n) -> p k n", k=KD)

        small_in = sem("small_in")
        bias_in = sem("bias_in")
        x_in = [sem(f"x_in{t}") for t in range(NT)]
        gdw_in = sem("gdw_in")
        lruw_in = sem("lruw_in")
        piece_in = [sem(f"piece_in{i}") for i in range(3)]
        tile_in = [sem(f"tile_in{i}") for i in range(4)]
        consts = sem("consts")
        smt_ready = sem("smt_ready")
        smt_out = sem("smt_out")
        cs_zero = sem("cs_zero")
        cs_ready = sem("cs_ready")
        mod_out = sem("mod_out")
        xhat_ready = sem("xhat_ready")
        product_ready = sem("product_ready")
        took = {"A": sem("act_took"), "D": sem("dve_took")}
        sums = sem("sums")
        roots = sem("roots")
        act_chain = sem("act_chain")
        dve_chain = sem("dve_chain")
        pool_chain = sem("pool_chain")
        xlp_zero = sem("xlp_zero")
        lam_exp = sem("lam_exp")
        lam_ready = sem("lam_ready")
        conv_ready = sem("conv_ready")
        lru_sqrt = sem("lru_sqrt")
        lru_done = sem("lru_done")
        att_zero = sem("att_zero")
        scan_mask = sem("scan_mask")
        zlog = sem("zlog")
        bready = sem("bready")
        diffs = sem("diffs")
        exps = sem("exps")
        qk_ready = sem("qk_ready")
        kd_ready = sem("kd_ready")
        qin_ready = sem("qin_ready")
        rd_ready = sem("rd_ready")
        sg_in = sem("sg_in")
        att_ready = sem("att_ready")
        oroot = sem("oroot")
        rowsT = sem("rowsT")
        rows_t_out = sem("rows_t_out")
        rows_out = sem("rows_out")
        rows_in = [sem(f"rows_in{i}") for i in range(2)]
        h2_ready = sem("h2_ready")
        h2_out = [sem(f"h2_out{i}") for i in range(2)]
        zrow_out = sem("zrow_out")
        lfin_ready = sem("lfin_ready")
        lfinT = sem("lfinT")
        lfin_t_out = sem("lfin_t_out")
        outs = sem("outs")
        logits_ready = sem("logits_ready")
        gexp = sem("gexp")
        gready = sem("gready")
        eexp = sem("eexp")
        eready = sem("eready")
        choice = sem("choice")
        ranks = sem("ranks")
        onehots = sem("onehots")
        tables = sem("tables")
        routed = sem("routed")
        e13_in = [sem(f"e13_in{i}") for i in range(4)]
        e2_in = [sem(f"e2_in{i}") for i in range(4)]
        gx_in = [sem(f"gx_in{i}") for i in range(2)]
        x_turned = sem("x_turned")
        x_taken = sem("x_taken")
        hid = sem("hid")
        silu = sem("silu")
        act_ready = sem("act_ready")
        a_turned = sem("a_turned")
        a_taken = sem("a_taken")
        y_done = sem("y_done")
        y_taken = sem("y_taken")
        y_out = [sem(f"y_out{i}") for i in range(2)]
        moe_done = sem("moe_done")
        ov = {n: sem("ov_" + n) for n in ("tok", "w", "gx", "xT", "xg", "hid", "silu", "act", "aT", "at", "y", "yt", "out", "sc")}
        ov_turns = sem("ov_turns")
        yg_in = [sem(f"yg_in{t}") for t in range(NT)]
        fg_in = sem("fg_in")
        pair_sum = sem("pair_sum")
        ready_out = sem("ready_out")

        sm_parts = [(c, KD), (c_ctx.rearrange("(a n) -> a n", a=1), KD), (norm1_g, KD), (norm2_g, KD), (conv_w[0], 4 * LC),
                    (conv_b, LC), (lru_br[0], 8), (lru_bi[0], 8), (lru_lam[0], 8), (gla_bg[0], 4),
                    (state_lru[0, 0], 8), (gla_norm_g, 1)]
        at, off = [], 0
        for _, n in sm_parts:
            at.append(off)
            off += n
        assert off == NSM
        C0, CX0, N1, N2, CW, CB, BR, BI, LAM, BG, H0, GN = at
        SMALL = 16 * len(sm_parts)
        BIASES = 16 * 6

        def wait_piece(eng, name):
            n = piece[name]
            eng.wait_ge(piece_in[n % 3], 16 * sum(m % 3 == n % 3 and pieces[m][0] not in tiled for m in range(n + 1)))

        def wait_tile(eng, name, i):
            eng.wait_ge(tile_in[i], 16 * (tiled[name][1] + 1))

        def count(name):
            who = order[place[name]][1]
            return who, sum(w == who for _, w in order[:place[name] + 1])

        def wait_taken(eng, name):
            who, n = count(name)
            eng.wait_ge(took[who], n)

        def small_part(n):
            src, rows_n = sm_parts[n]
            if len(src.shape) == 2:
                src = src.rearrange("a (b n) -> (a b) n", n=P if rows_n > 1 else src.shape[-1])
            return sm_in[at[n]:at[n] + rows_n, :], src

        def halves(ap):
            return ap[:, 0:NS], ap[:, NS:N]

        block = ctx.enter_context(nc.Block())

        @block.sync
        def _(sp):
            def load_piece(name):
                n = piece[name]
                dst = wring[:, n % 3, :].rearrange("p (k n) -> p k n", k=KD)
                if name in tiled:
                    for i in range(4):
                        sp.wait_ge(product_ready, place[tiled[name][0][i]] + 1)
                        cols = slice(i * P, (i + 1) * P)
                        sp.dma_start(dst[:, :, cols], pieces[n][1][:, :, cols]).then_inc(tile_in[i], 16)
                    return
                if n >= 3:
                    old = pieces[n - 3][0]
                    use = f"ad{old[1:]}" if old[0] == "a" else last_use[old]
                    sp.wait_ge(product_ready, place[use] + 1)
                sp.dma_start(dst, pieces[n][1]).then_inc(piece_in[n % 3], 16)

            load_piece("a0")
            for n in range(len(sm_parts) // 2):
                sp.dma_start(*small_part(n)).then_inc(small_in, 16)
            load_piece("a1")
            for t in range(NT):
                src = x_s[t * P:t * P + P, :] if t < ST else x_p[(t - ST) * P:(t - ST) * P + P, :]
                sp.dma_start(xres[:, t, :], src).then_inc(x_in[t], 16)
            for n in range(2, 6):
                load_piece(pieces[n][0])
            sp.dma_start(wgd[:, :, :], wi[:, :, GD0:GD0 + 2 * RANK]).then_inc(gdw_in, 16)
            sp.wait_ge(consts, 2)
            sp.dma_start(h2_d[N, :].rearrange("(k n) -> k n", n=P), zero[0:KD, :]).then_inc(zrow_out, 16)
            for s in range(2):
                sp.dma_start(wgb[s * RANK:(s + 1) * RANK, s * QK:(s + 1) * QK], gla_wg[0, s]).then_inc(bias_in, 16)
            sp.dma_start(rbias[:, 0:NG], router_gb.to_broadcast([P, NG])).then_inc(bias_in, 16)
            sp.dma_start(rbias[:, NG:], router_eb.to_broadcast([P, NE])).then_inc(bias_in, 16)
            sp.dma_start(rw[:, :, 0:NG], router_gw[0].rearrange("(k p) n -> p k n", p=P)).then_inc(bias_in, 16)
            sp.dma_start(rw[:, :, NG:], router_ew[0].rearrange("(k p) n -> p k n", p=P)).then_inc(bias_in, 16)
            for wn, src in enumerate((lru_wr, lru_wi)):
                for s in range(2):
                    blocks = src[0, s].rearrange("(c h) a b -> h a c b", h=2)
                    for half in range(2):
                        sp.dma_start(lruw[half * LB:(half + 1) * LB, wn, s, :, half * LB:(half + 1) * LB],
                                     blocks[half]).then_inc(lruw_in, 16)
            for n in range(6, 17):
                load_piece(pieces[n][0])
                if n >= 8:
                    u = n - 8
                    sp.dma_start(y_d[(NE + u) * P:(NE + u + 1) * P, :].rearrange("p (k n) -> p k n", n=P),
                                 zero[:, :].rearrange("p (a n) -> p a n", a=1).to_broadcast([P, KD, P])).then_inc(zrow_out, 16)
            wait_taken(sp, "aT11")
            for s in range(2):
                for t in range(QT):
                    sp.dma_start(sg0[:, 2 * t + s, :], state_gla[0, 0, s, 2 * t:2 * t + 2].rearrange("h k v -> (h k) v")) \
                        .then_inc(sg_in, 16)
            sp.wait_ge(rows_t_out, 1)
            sp.dma_start(rows_d.rearrange("(r n) -> r n", n=P), rows_t[:, :]).then_inc(rows_out, 16)
            load_piece("wo0")
            load_piece("wo1")
            sp.wait_ge(rows_out, 16)
            sp.wait_ge(qk_ready, 4)
            wait_taken(sp, "at31")
            wait_taken(sp, "kT3")

            def load_row(seq, kind):
                i = 4 * seq + kind
                sp.dma_start(rows[seq][kind], rows_d[i * D:(i + 1) * D].rearrange("(a n) -> a n", a=1).to_broadcast([P, D])) \
                    .then_inc(rows_in[seq], 16)

            for kind in range(4):
                load_row(0, kind)
            wait_taken(sp, "kvB3")
            for s in range(2):
                for t in range(QT):
                    sp.dma_start(state_gla_new[0, 0, s, 2 * t:2 * t + 2].rearrange("h k v -> (h k) v"), sfin[:, 2 * t + s, :]) \
                        .then_inc(outs, 16)
            wait_taken(sp, f"oT{NT - 1}")
            for kind in range(4):
                load_row(1, kind)
            sp.wait_ge(lfin_t_out, 1)
            sp.dma_start(state_lru_new[0, 0].rearrange("s (c n) -> (s c) n", n=P), lfin_t[:, :]).then_inc(outs, 16)

            def load13(u):
                w = exp_w13[0, u].rearrange("(k p) f -> p k f", p=P)
                sp.dma_start(e13[u % 4], w).then_inc(e13_in[u % 4], 16)

            def load2(u):
                w = exp_w2[0, u].rearrange("(k p) f -> p k f", p=P)
                sp.dma_start(e2[u % 4], w).then_inc(e2_in[u % 4], 16)

            load13(0)
            load2(0)
            load13(1)
            for t in range(NT):
                sp.wait_ge(h2_ready, t + 1)
                sp.dma_start(h2_d[t * P:(t + 1) * P, :], h2[:, t % 2, :]).then_inc(h2_out[t % 2], 16)
            wait_taken(sp, "mx4")
            load2(1)
            load13(2)
            load2(2)
            sp.wait_ge(logits_ready, NT)
            for i in range(2):
                sp.wait_ge(h2_out[i], 16 * ((NT - i + 1) // 2))
            load13(3)
            load2(3)
            for u in range(4, NE):
                sp.wait_ge(hid, u - 3)
                load13(u)
                sp.wait_ge(y_done, 2 * (u - 3))
                load2(u)

            sp.wait_ge(hid, NE - 1)
            sp.dma_start(fing, final_g.rearrange("(a n) -> a n", a=1).to_broadcast([P, D])).then_inc(fg_in, 16)

            sp.wait_ge(moe_done, 1)
            n_over = sp.value_load(eidi[0:1, NOV:NOV + 1], min_val=0, max_val=NOV)
            with sp.If(n_over > 0):
                with sp.Fori(0, NOV) as i:
                    with sp.If(n_over > i):
                        e = sp.value_load(eidi[0:1, bass.ds(i, 1)], min_val=0, max_val=NE - 1)
                        sp.dma_start(e13[0], exp_w13[0, bass.ds(e, 1)].rearrange("a (k p) f -> p (a k) f", p=P)).then_inc(ov["w"], 16)
                        sp.dma_start(e2[0], exp_w2[0, bass.ds(e, 1)].rearrange("a (k p) f -> p (a k) f", p=P)).then_inc(ov["w"], 16)
                        sp.wait_ge(ov["yt"], i + 1)
                        sp.dma_start(y_d[bass.ds((i + NE) * P, P), :], ysb[:, 0, :]).then_inc(ov["out"], 16)
                        sp.wait_ge(ov["out"], (i + 1) * 16)
                        sp.sem_inc(ov_turns, 1)
                    sp.nop()
            for t in range(NT):
                sp.wait_ge(ready_out, t + 1)
                dst = y_sample[0, t * P:t * P + P, :] if t < ST else y_prompt[0, (t - ST) * P:(t - ST) * P + P, :]
                sp.dma_start(dst, xres[:, t, :]).then_inc(outs, 16)
            sp.wait_ge(outs, 16 * (4 + 1 + NT))

        @block.gpsimd
        def _(pool):
            n_chain = [0]

            def link(ins):
                n_chain[0] += 1
                ins.then_inc(pool_chain, 1)
                pool.wait_ge(pool_chain, n_chain[0])

            nc.gpsimd.memset(cs[:, :, :], 0.0).then_inc(cs_zero, 1)
            link(nc.gpsimd.memset(ident[:, :], 0.0))
            nc.gpsimd.affine_select(out=ident[:, :], in_=ident[:, :], compare_op=ALU.not_equal, fill=1.0, base=0,
                                    pattern=[[-1, P]], channel_multiplier=1).then_inc(consts, 1)
            nc.gpsimd.memset(eps[:, :], EPS)
            nc.gpsimd.memset(zero[:, :], 0.0)
            nc.gpsimd.memset(wgb[:, :], 0.0)
            link(nc.gpsimd.memset(ones[:, :], 1.0))
            nc.gpsimd.memset(lruw[:, :, :, :, :].rearrange("p w s c n -> p (w s c n)"), 0.0).then_inc(consts, 1)
            nc.gpsimd.memset(xlp[:, :, 0:PADS].rearrange("p c (r w) -> p c r w", w=PAD)[:, :, :, 0:2], 0.0)
            nc.gpsimd.memset(xlp[:, :, 0:PADS].rearrange("p c (r w) -> p c r w", w=PAD)[:, :, :, PAD - 1:PAD], 0.0)
            nc.gpsimd.memset(xlp[:, :, PADS:PADS + 2], 0.0)
            nc.gpsimd.memset(xlp[:, :, XLP - 1:XLP], 0.0).then_inc(xlp_zero, 1)
            nc.gpsimd.affine_select(out=before[:, :], in_=ones[:, :], compare_op=ALU.is_gt, fill=0.0, base=0,
                                    pattern=[[1, P]], channel_multiplier=-1)
            nc.gpsimd.affine_select(out=mask[:, 0, :], in_=ones[:, :], compare_op=ALU.is_ge, fill=0.0, base=0,
                                    pattern=[[1, P]], channel_multiplier=-1)
            link(nc.gpsimd.affine_select(out=mask[:, 1, :], in_=ones[:, :], compare_op=ALU.is_ge, fill=0.0, base=0,
                                         pattern=[[-1, P]], channel_multiplier=1))
            link(nc.gpsimd.memset(mask[0:CHUNK, 0, CHUNK:P], 0.0))
            link(nc.gpsimd.memset(mask[CHUNK:P, 1, 0:CHUNK], 0.0))
            nc.gpsimd.iota(numbers[:, :], pattern=[[1, P]], base=0, channel_multiplier=0, allow_small_or_imprecise_dtypes=True)
            nc.gpsimd.iota(w4[:, :], pattern=[[-1, NG]], base=NG, channel_multiplier=0, allow_small_or_imprecise_dtypes=True)
            nc.gpsimd.iota(thresholds[:, :], pattern=[[P, NT - 1]], base=P, channel_multiplier=0, allow_small_or_imprecise_dtypes=True)
            nc.gpsimd.iota(tokid[:, :], pattern=[[P, NT]], base=-N, channel_multiplier=1, allow_small_or_imprecise_dtypes=True) \
                .then_inc(consts, 1)
            pool.wait_ge(lru_done, 2)
            nc.gpsimd.memset(attb[:, :], 0.0)
            nc.gpsimd.memset(tmp[:, 18 * N:22 * N], 0.0).then_inc(att_zero, 1)
            wait_taken(pool, "g3")
            link(nc.gpsimd.memset(gd[:, :], 1.0))
            nc.gpsimd.memset(gd[:, :].rearrange("p (c i) -> p c i", i=CHUNK)[:, :, 0:1], 0.0).then_inc(scan_mask, 1)
            wait_taken(pool, "q1")
            for g in range(4):
                r = 3 * (g % 2)
                last = CHUNK - 1 if g % 2 == 0 else 0
                pool.wait_ge(exps, g + 1)
                nc.gpsimd.tensor_tensor(gt[:, r + 2, :], gt[:, r + 2, :], kk[:, g // 2, :], ALU.mult).then_inc(kd_ready, 1)
                link(nc.gpsimd.tensor_copy(dec[:, g, :], qin[:, g, :].rearrange("p (c i) -> p c i", i=CHUNK)[:, :, last]))
                nc.gpsimd.tensor_tensor(qin[:, g, :], qin[:, g, :], q[:, g // 2, :], ALU.mult).then_inc(qin_ready, 1)

            def gather(u):
                b = u % 2
                if u >= 2:
                    pool.wait_ge(x_turned, u - 1)
                pool.indirect_dma_start(gx[:, b, :], None, h2_d[:, :],
                                        bass.IndirectOffsetOnAxis(ap=slot_tok[:, u:u + 1].bitcast(U32), axis=0)) \
                    .then_inc(gx_in[b], 16)

            pool.wait_ge(routed, 1)
            for i in range(2):
                pool.wait_ge(h2_out[i], 16 * ((NT - i + 1) // 2))
            pool.wait_ge(zrow_out, 16 * (1 + NOV))
            for u in range(NE):
                gather(u)
            n_over = pool.value_load(eidi[0:1, NOV:NOV + 1], min_val=0, max_val=NOV)
            pool.wait_ge(moe_done, 1)
            with pool.If(n_over > 0):
                with pool.Fori(0, NOV) as i:
                    with pool.If(n_over > i):
                        pool.wait_ge(ov["tok"], i + 1)
                        pool.sem_inc(ov_turns, 1)
                        pool.indirect_dma_start(gx[:, 0, :], None, h2_d[:, :],
                                                bass.IndirectOffsetOnAxis(ap=ov_tok[:, 0:1].bitcast(U32), axis=0)) \
                            .then_inc(ov["gx"], 16)
                        pool.wait_ge(ov["out"], (i + 1) * 16)
                        pool.sem_inc(ov_turns, 1)
                    pool.nop()
            for i in range(2):
                pool.wait_ge(y_out[i], 16 * NE // 2)
            for t in range(NT):
                for j in range(2):
                    pool.indirect_dma_start(yg[:, 2 * t + j, :], None, y_d[:, :],
                                            bass.IndirectOffsetOnAxis(ap=yidx[:, j * NT + t:j * NT + t + 1].bitcast(U32), axis=0)) \
                        .then_inc(yg_in[t], 16)

        @block.scalar
        def _(act):
            A = nc.scalar.activation
            n_chain = [0]

            def chain(ins):
                n_chain[0] += 1
                ins.then_inc(act_chain, 1)

            def settle():
                act.wait_ge(act_chain, n_chain[0])

            def ready(name):
                act.wait_ge(product_ready, place[name] + 1)
                return product(name)

            for n in range(len(sm_parts) // 2, len(sm_parts)):
                act.dma_start(*small_part(n)).then_inc(small_in, 16)
            act.dma_start(adab_in, ada_b.rearrange("a (m n) -> (a m) n", n=P)).then_inc(small_in, 16)
            act.wait_ge(cs_zero, 1)
            act.wait_ge(smt_out, 1)
            A(cs[:, :, 0], smT[:, C0:C0 + KD], ACT.Silu)
            A(cs[:, :, 1], smT[:, CX0:CX0 + KD], ACT.Silu).then_inc(cs_ready, 1)

            def take_mod(j):
                if j >= 2:
                    act.wait_ge(product_ready, place[f"aT{j - 2}"] + 1)
                A(adrow[j % 2], ready(f"ad{j}")[:, 0:512], ACT.Copy).then_inc(took["A"], 1)

            take_mod(0)
            take_mod(1)
            for t in range(NT):
                act.wait_ge(x_in[t], 16)
                i = A(junk[:, t, :], xres[:, t, :], ACT.Square, accum_out=st[:, 0, t:t + 1])
            i.then_inc(sums, 1)
            act.wait_ge(sums, 1)
            act.wait_ge(consts, 2)
            A(st[:, 2, :], st[:, 0, :], ACT.Sqrt, bias=eps[:, 0:1], scale=1 / D).then_inc(roots, 1)
            chain(A(lam[:, 0, :], smT[:, LAM:LAM + 8], ACT.Abs))
            settle()
            A(lam[:, 1, :], lam[:, 0, :], ACT.Exp, scale=-1.0).then_inc(lam_exp, 1)
            chain(A(hb[:, :], smT[:, BR:BR + 16], ACT.Copy, scale=0.5))
            take_mod(2)
            take_mod(3)
            act.wait_ge(mod_out, 1)
            for k in range(0, KD, 2):
                src = ready(f"xT{k}")
                A(hT[:, k, 0:NS], src[:, 0:NS], ACT.Identity, bias=mod[:, k, 0:1], scale=A1[:, k, 0:1])
                A(hT[:, k, NS:N], src[:, NS:N], ACT.Identity, bias=mod[:, k, 1:2], scale=A1[:, k, 1:2]).then_inc(took["A"], 1)
            act.wait_ge(xlp_zero, 1)
            for t in range(LC):
                src = ready(f"xl{t}")
                A(xlp[:, t, 0:PADS].rearrange("p (r w) -> p r w", w=PAD)[:, :, 2:PAD - 1],
                  src[:, 0:NS].rearrange("p (r w) -> p r w", w=GRID_W), ACT.Copy)
                A(xlp[:, t, PADS + 2:XLP - 1], src[:, NS:N], ACT.Copy).then_inc(took["A"], 1)
            take_mod(4)
            take_mod(5)
            act.wait_ge(lam_ready, 1)
            for h in range(2):
                if h:
                    act.wait_ge(lru_done, h)
                for j in range(4):
                    ch, s = 2 * h + j // 2, j % 2
                    for w, dst in enumerate((tau, ix)):
                        b = 8 * w + 4 * s + ch
                        A(dst[:, j, :], ready(f"lr{ch}{s}{w}")[:, 0:N], ACT.Tanh, bias=hb[:, b:b + 1], scale=0.5) \
                            .then_inc(took["A"], 1)
                    if h == 0:
                        A(mixT[:, j, :], ready(f"yl{j}")[:, 0:N], ACT.Gelu_apprx_tanh).then_inc(took["A"], 1)
                    else:
                        A(v[:, j, :], ready(f"v{j}")[:, 0:512], ACT.Copy).then_inc(took["A"], 1)
                if h == 0:
                    take_mod(6)
                    take_mod(7)
                act.wait_ge(took["A"], count(f"lr{2 * h + 1}11")[1])
                for j in range(4):
                    m = 4 * (j % 2) + 2 * h + j // 2
                    A(av[:, j, :], tau[:, j, :], ACT.Exp, bias=lam[:, 3, m:m + 1], scale=lam[:, 3, m:m + 1])
                    chain(A(tau[:, j, :], tau[:, j, :], ACT.Tanh, bias=lam[:, 4, m:m + 1], scale=lam[:, 4, m:m + 1]))
                settle()
                for j in range(4):
                    A(tau[:, j, :], tau[:, j, :], ACT.Sqrt, scale=0.25).then_inc(lru_sqrt, 1)
                if h == 0:
                    for t in range(QT):
                        A(kk[:, t, :], ready(f"k{t}")[:, 0:N], ACT.Copy).then_inc(took["A"], 1)
                    for t in range(QT):
                        A(q[:, t, :], ready(f"q{t}")[:, 0:N], ACT.Copy, scale=DK ** -0.5).then_inc(took["A"], 1)
                    A(gd[0:2 * RANK, :], ready("gd")[0:2 * RANK, 0:N], ACT.Copy).then_inc(took["A"], 1)
                    take_mod(8)
                    take_mod(9)
            A(v[:, 4, :], ready("v4")[:, 0:512], ACT.Copy).then_inc(took["A"], 1)
            take_mod(10)
            take_mod(11)
            def take_og(h):
                A(mixT[:, LC + h, :], ready(f"og{h}")[:, 0:N], ACT.Copy).then_inc(took["A"], 1)

            take_og(0)
            act.wait_ge(lru_done, 2)
            for g in range(4):
                b = BG + 2 * (g % 2) + g // 2
                A(bcum[:, g, :], ready(f"g{g}")[:, 0:N], ACT.Identity, bias=smT[:, b:b + 1]).then_inc(took["A"], 1)
            for g in range(4):
                act.wait_ge(took["A"], count(f"g{g}")[1])
                chain(A(gt[:, g, :], bcum[:, g, :], ACT.Abs))
            settle()
            for g in range(4):
                chain(A(gt[:, g, :], gt[:, g, :], ACT.Exp, scale=-1.0))
            settle()
            for g in range(4):
                A(gt[:, g, :], gt[:, g, :], ACT.Ln, bias=1.0).then_inc(zlog, 1)
            take_og(1)

            def exponentials(g):
                r = 3 * (g % 2)
                act.wait_ge(diffs, g + 1)
                A(qin[:, g, :], bcum[:, g, :], ACT.Exp, scale=1 / GLA_TAU)
                chain(A(gt[:, r + 1, :], gt[:, r, :], ACT.Exp, scale=-1 / GLA_TAU))
                A(gt[:, r, :], gt[:, r, :], ACT.Exp, scale=1 / GLA_TAU)
                A(gt[:, r + 2, :], gt[:, r + 2, :], ACT.Exp, scale=1 / GLA_TAU).then_inc(exps, 1)

            def take_kT(g):
                A(kdT[:, g, :], ready(f"kT{g}")[:, 0:N], ACT.Copy).then_inc(took["A"], 1)

            exponentials(0)
            take_og(2)
            exponentials(1)
            take_kT(0)
            take_og(3)
            exponentials(2)
            take_kT(1)
            exponentials(3)
            take_kT(2)
            act.wait_ge(took["A"], count("og3")[1])
            for h in range(HEADS):
                chain(A(mixT[:, LC + h, :], mixT[:, LC + h, :], ACT.Silu))
            take_kT(3)
            settle()
            wait_taken(act, "kvB3")
            for t in range(NT):
                src = ready(f"o{t}")
                for h in range(HEADS):
                    col = (h % 2) * 512 + (h // 2) * DV
                    chain(A(osq[:, h * DV:(h + 1) * DV], src[:, col:col + DV], ACT.Square, accum_out=orms[:, 0, t, h:h + 1]))
                settle()
                A(orms[:, 1, t, :], orms[:, 0, t, :], ACT.Sqrt, bias=eps[:, 0:1], scale=1 / DV).then_inc(oroot, 1)
            def take_rows(t):
                if t >= 2:
                    act.wait_ge(logits_ready, t - 1)
                A(h2T[:, t % 2, :, :].rearrange("p k n -> p (k n)"), ready(f"hh{t}"), ACT.Copy).then_inc(took["A"], 1)

            for t in range(NT):
                if t:
                    take_rows(t - 1)
                act.wait_ge(rd_ready, t + 1)
                A(mtmp, xres[:, t, :], ACT.Square, accum_out=st[:, 3, t:t + 1]).then_inc(sums, 1)
                act.wait_ge(sums, 2 + t)
                A(rt[:, 1, t:t + 1], st[:, 3, t:t + 1], ACT.Sqrt, bias=eps[:, 0:1], scale=1 / D).then_inc(roots, 1)
            take_rows(NT - 1)
            act.wait_ge(gready, 1)
            A(r4[:, 1, :, :], r4[:, 0, :, :], ACT.Exp).then_inc(gexp, 1)
            act.wait_ge(eready, 1)
            A(r4[:, 4, :, :], r4[:, 3, :, :], ACT.Exp).then_inc(eexp, 1)

            def silu_of(u):
                act.wait_ge(hid, u + 1)
                if u >= 2:
                    act.wait_ge(act_ready, u - 1)
                A(sact[:, u % 2, :], ms[:, u % 2, 0:DE], ACT.Silu).then_inc(silu, 1)

            silu_of(0)
            for u in range(NE):
                if u + 1 < NE:
                    silu_of(u + 1)
                b = u % 2
                if u >= 2:
                    act.wait_ge(y_out[b], 16 * (u // 2))
                for h in range(2):
                    act.wait_ge(y_done, 2 * u + h + 1)
                    A(ysb[:, b, h * 512:(h + 1) * 512], ps[:, 2, h * 512:(h + 1) * 512], ACT.Copy).then_inc(y_taken, 1)
                act.wait_ge(y_taken, 2 * u + 2)
                act.dma_start(y_d[u * P:(u + 1) * P, :], ysb[:, b, :]).then_inc(y_out[b], 16)
            n_over = act.value_load(eidi[0:1, NOV:NOV + 1], min_val=0, max_val=NOV)
            for i in range(2):
                act.wait_ge(y_out[i], 16 * NE // 2)
            act.sem_inc(moe_done, 1)
            with act.If(n_over > 0):
                with act.Fori(0, NOV) as i:
                    with act.If(n_over > i):
                        act.wait_ge(ov["hid"], i + 1)
                        A(sact[:, 0, :], ms[:, 0, 0:DE], ACT.Silu).then_inc(ov["silu"], 1)
                        act.wait_ge(ov["y"], i + 1)
                        A(ysb[:, 0, :], ps[:, 2, :], ACT.Copy).then_inc(ov["yt"], 1)
                        act.wait_ge(ov["out"], (i + 1) * 16)
                        act.sem_inc(ov_turns, 1)
                    act.nop()
            for t in range(NT):
                act.wait_ge(rd_ready, NT + t + 1)
                A(yg[:, 2 * t + 1, :], xres[:, t, :], ACT.Square, accum_out=st[:, 0, t:t + 1]).then_inc(sums, 1)
                act.wait_ge(sums, 2 + NT + t)
                A(st[:, 2, t:t + 1], st[:, 0, t:t + 1], ACT.Sqrt, bias=eps[:, 0:1], scale=1 / D).then_inc(roots, 1)

        @block.tensor
        def _(pe):
            mm = nc.tensor.matmul

            def start(name):
                n = place[name]
                if n >= RING:
                    wait_taken(pe, order[n - RING][0])
                return product(name)

            def wide(dst, lhsT, rhs, first, last):
                for d, r in zip(halves(dst), halves(rhs)):
                    i = mm(d, lhsT, r, start=first, stop=last)
                return i

            pe.wait_ge(consts, 1)
            pe.wait_ge(small_in, SMALL + 16)
            nc.tensor.transpose(ms[:, 0, 0:NSM], sm_in[0:NSM, :], ident[0:NSM, 0:NSM])
            nc.tensor.transpose(ms[:, 0, P:P + 6 * KD], adab_in, ident[0:6 * KD, 0:6 * KD]).then_inc(smt_ready, 1)

            def modulation(j):
                dst = start(f"ad{j}")
                wait_piece(pe, f"a{j}")
                w = weights(f"a{j}")
                for k in range(KD):
                    r = 32 * (k % 4)
                    i = mm(dst[r:r + 32, 0:512], cs[:, k, :], w[:, k, :], start=(k < 4), stop=(k >= 4), skip_group_check=True)
                i.then_inc(product_ready, 1)

            def turn_modulation(j):
                dst = start(f"aT{j}")
                wait_taken(pe, f"ad{j}")
                for m in range(4):
                    i = nc.tensor.transpose(dst[:, m * P:(m + 1) * P], adrow[j % 2][:, m * P:(m + 1) * P], ident[:, :])
                i.then_inc(product_ready, 1)

            def two_of(f, j):
                f(j)
                f(j + 1)

            pe.wait_ge(cs_ready, 1)
            for j in range(4):
                modulation(j)
                if j:
                    turn_modulation(j - 1)
            turn_modulation(3)
            pe.wait_ge(xhat_ready, 1)
            for k in range(KD):
                dst = start(f"xT{k}")
                for t in range(NT):
                    i = nc.tensor.transpose(dst[:, t * P:(t + 1) * P], xhat[:, t, k * P:(k + 1) * P], ident[:, :])
                i.then_inc(product_ready, 1)
            wait_taken(pe, f"xT{KD - 1}")
            wait_taken(pe, f"xT{KD - 2}")

            def project(name, w, col, rows=P):
                dst = start(name)
                for k in range(KD):
                    i = wide(dst[0:rows, :], w[:, k, col:col + rows], hT[:, k, :], k == 0, k == KD - 1)
                i.then_inc(product_ready, 1)
                return i

            def gates(ch, s):
                pe.wait_ge(conv_ready, ch + 1)
                for w in range(2):
                    wide(start(f"lr{ch}{s}{w}"), lruw[:, w, s, ch, :], xc[:, ch, :], True, True).then_inc(product_ready, 1)

            def values(t):
                dst = start(f"v{t}")
                w = weights("v")
                for k in range(KD):
                    i = mm(dst[:, 0:512], hT[:, k, t * P:(t + 1) * P], w[:, k, :], start=(k == 0), stop=(k == KD - 1))
                i.then_inc(product_ready, 1)

            wait_piece(pe, "xl")
            for t in range(LC):
                project(f"xl{t}", weights("xl"), t * P)
            two_of(modulation, 4)
            pe.wait_ge(lruw_in, 16 * 8)
            for n in range(4):
                gates(n // 2, n % 2)
                wait_tile(pe, "yl", n)
                project(f"yl{n}", weights("yl"), n * P)
                if n == 0:
                    two_of(turn_modulation, 4)
            two_of(modulation, 6)
            two_of(turn_modulation, 6)
            for t in range(QT):
                wait_tile(pe, "qk", QT + t)
                project(f"k{t}", weights("qk"), QK + t * P)
            for t in range(QT):
                wait_tile(pe, "qk", t)
                project(f"q{t}", weights("qk"), t * P)
            pe.wait_ge(gdw_in, 16)
            project("gd", wgd, 0, 2 * RANK)
            two_of(modulation, 8)
            wait_piece(pe, "v")
            for n in range(4):
                gates(2 + n // 2, n % 2)
                values(n)
                if n == 0:
                    two_of(turn_modulation, 8)
            values(4)
            two_of(modulation, 10)
            wait_tile(pe, "og", 0)
            project("og0", weights("og"), 0)
            two_of(turn_modulation, 10)
            pe.wait_ge(bias_in, BIASES)
            wait_taken(pe, "gd")
            for g in range(4):
                col = (g % 2) * QK + (g // 2) * P
                wide(start(f"g{g}"), wgb[:, col:col + P], gd[0:2 * RANK, :], True, True).then_inc(product_ready, 1)
            wait_tile(pe, "og", 1)
            project("og1", weights("og"), P)
            for g in range(4):
                r = 3 * (g % 2)
                tt = g // 2
                if g == 0:
                    wait_tile(pe, "og", 2)
                    project("og2", weights("og"), 2 * P)
                pe.wait_ge(kd_ready, g + 1)
                dst = start(f"kT{g}")
                for t in range(NT):
                    i = nc.tensor.transpose(dst[:, t * P:(t + 1) * P], gt[:, r + 2, t * P:(t + 1) * P], ident[:, :])
                i.then_inc(product_ready, 1)
                pe.wait_ge(qk_ready, g + 1)
                for hh in range(2):
                    dst = start(f"at{g}{hh}")
                    rows_h = slice(hh * DK, (hh + 1) * DK)
                    for t in range(NT):
                        cols = slice(t * P, (t + 1) * P)
                        i = mm(dst[:, cols], gt[rows_h, r + 1, cols], gt[rows_h, r, cols], start=True, stop=True)
                    i.then_inc(product_ready, 1)
                if g == 0:
                    wait_tile(pe, "og", 3)
                    project("og3", weights("og"), 3 * P)
                    pe.wait_ge(mod_out, 2)
                    nc.tensor.transpose(ms[0:8 * KD, 0, 0:P], A2[:, :, :].rearrange("p a k -> p (a k)"), ident[:, :]).then_inc(rowsT, 1)
                    pe.wait_ge(lfin_ready, 8)
                    nc.tensor.transpose(ms[0:8, 0, P:2 * P], lfin[:, :], ident[:, :]).then_inc(lfinT, 1)
                wait_taken(pe, f"kT{g}")
                for name, chunks in ((f"kvA{g}", range(SC)), (f"kvB{g}", range(SC, NC))):
                    dst = start(name)
                    for cn in chunks:
                        half = slice((cn % 2) * CHUNK, (cn % 2 + 1) * CHUNK)
                        col = (cn % 2) * 512 + (cn - chunks[0]) // 2 * DV
                        t = cn // 2
                        for hh in range(2):
                            h = 2 * tt + hh
                            i = mm(dst[hh * DK:(hh + 1) * DK, col:col + DV],
                                   kdT[half, g, t * P + hh * DK:t * P + (hh + 1) * DK], v[half, t, h * DV:(h + 1) * DV],
                                   start=True, stop=True)
                    i.then_inc(product_ready, 1)
            pe.wait_ge(sg_in, 16 * 4)
            wait_taken(pe, "kvB3")
            pe.wait_ge(qin_ready, 4)
            pe.wait_ge(att_ready, HEADS)

            def attend(t):
                dst = start(f"o{t}")
                cols = slice(t * P, (t + 1) * P)
                for h in range(HEADS):
                    tt, hh = h // 2, h % 2
                    rows_h = slice(hh * DK, (hh + 1) * DK)
                    out = slice(hh * 512 + tt * DV, hh * 512 + (tt + 1) * DV)
                    mm(dst[:, out], att[:, h, cols], v[:, t, h * DV:(h + 1) * DV], start=True, stop=False, skip_group_check=True)
                    parts = []
                    for cn in (2 * t, 2 * t + 1):
                        for s in range(2):
                            if cn >= SC and cn == (SC if s == 0 else NC - 1):
                                continue
                            first = cn == (0 if s == 0 else SC - 1)
                            parts.append((cn, s, sg0[rows_h, 2 * tt + s, :] if first else S[rows_h, 2 * tt + s, cn, :]))
                    for n, (cn, s, state) in enumerate(parts):
                        r = (cn % 2) * CHUNK
                        i = mm(dst[r:r + CHUNK, out], qin[rows_h, 2 * tt + s, cn * CHUNK:(cn + 1) * CHUNK], state, start=False,
                               stop=(n == len(parts) - 1), skip_group_check=True)
                i.then_inc(product_ready, 1)

            def turn_o(t):
                dst = start(f"oT{t}")
                wait_taken(pe, f"o{t}")
                for h in range(HEADS):
                    i = nc.tensor.transpose(dst[:, h * P:(h + 1) * P], otok[:, t % 2, h * DV:(h + 1) * DV], ident[:, :])
                i.then_inc(product_ready, 1)

            for t in range(NT):
                attend(t)
                if t:
                    turn_o(t - 1)

            def turn_rows(t):
                pe.wait_ge(h2_ready, t + 1)
                dst = start(f"hh{t}")
                for k in range(KD):
                    i = nc.tensor.transpose(dst[:, k * P:(k + 1) * P], h2[:, t % 2, k * P:(k + 1) * P], ident[:, :])
                i.then_inc(product_ready, 1)

            def router(t):
                wait_taken(pe, f"hh{t}")
                for k in range(KD):
                    i = mm(ms[:, 0, t * (NG + NE):(t + 1) * (NG + NE)], h2T[:, t % 2, k, :], rw[:, k, :],
                           start=(k == 0), stop=(k == KD - 1))
                i.then_inc(logits_ready, 1)

            wait_piece(pe, "wo0")
            wait_piece(pe, "wo1")
            pe.wait_ge(rows_t_out, 1)
            pe.wait_ge(lfin_t_out, 1)
            pe.wait_ge(lru_done, 2)
            for t in range(NT):
                wait_taken(pe, f"oT{t}")
                dst = start(f"mx{t}")
                for half in range(2):
                    w = weights(f"wo{half}")
                    for k in range(KD):
                        i = mm(dst[:, half * 512:(half + 1) * 512], mixT[:, k, t * P:(t + 1) * P], w[:, k, :],
                               start=(k == 0), stop=(k == KD - 1))
                i.then_inc(product_ready, 1)
                if t == 0:
                    turn_o(NT - 1)
                if t:
                    turn_rows(t - 1)
                if t >= 2:
                    router(t - 2)
            router(NT - 2)
            turn_rows(NT - 1)
            router(NT - 1)
            pe.wait_ge(choice, 1)
            pe.wait_ge(consts, 3)
            chosen = r16[:, 2, :, :]
            flat = chosen.rearrange("p t e -> p (t e)")
            mm(ms[:, 1, 128:128 + NT * NE], before[:, :], flat, start=True, stop=False, skip_group_check=True)
            for back in range(1, NT):
                mm(ms[:, 1, 128 + back * NE:128 + NT * NE], ones[:, :], flat[:, 0:(NT - back) * NE], start=False,
                   stop=(back == NT - 1), skip_group_check=True)
            mm(ms[:, 1, 256:256 + NT * NE], ones[:, :], flat, start=True, stop=True, skip_group_check=True).then_inc(ranks, 1)
            pe.wait_ge(onehots, 1)
            for n in range(2 * NT):
                i = mm(ms[:, 0, 128:128 + 2 * NU], sel_a[:, n, :], sel_b[:, n, :], start=(n == 0), stop=(n == 2 * NT - 1))
            i.then_inc(tables, 1)

            def turn_x(u):
                b = u % 2
                pe.wait_ge(gx_in[b], 16 * (u // 2 + 1))
                if u:
                    pe.wait_ge(x_taken, u)
                for k in range(KD):
                    i = nc.tensor.transpose(ps[:, 0, k * P:(k + 1) * P], gx[:, b, k * P:(k + 1) * P], ident[:, :])
                i.then_inc(x_turned, 1)

            def hidden(u):
                b = u % 2
                pe.wait_ge(x_taken, u + 1)
                pe.wait_ge(e13_in[u % 4], 16 * (u // 4 + 1))
                if u >= 2:
                    pe.wait_ge(act_ready, u - 1)
                for k in range(KD):
                    i = mm(ms[:, b, :], xgT[:, b, k, :], e13[u % 4][:, k, :], start=(k == 0), stop=(k == KD - 1))
                i.then_inc(hid, 1)

            def turn_a(u):
                b = u % 2
                pe.wait_ge(act_ready, u + 1)
                if u:
                    pe.wait_ge(a_taken, u)
                for k in range(DC):
                    i = nc.tensor.transpose(ps[:, 1, k * P:(k + 1) * P], act_sb[:, b, k * P:(k + 1) * P], ident[:, :])
                i.then_inc(a_turned, 1)

            def output(u):
                b = u % 2
                pe.wait_ge(a_taken, u + 1)
                pe.wait_ge(e2_in[u % 4], 16 * (u // 4 + 1))
                for half in range(2):
                    if u:
                        pe.wait_ge(y_taken, 2 * u - 1 + half)
                    for k in range(DC):
                        i = mm(ps[:, 2, half * 512:(half + 1) * 512], aT[:, b, k, :], e2[u % 4][:, k, half * 512:(half + 1) * 512],
                               start=(k == 0), stop=(k == DC - 1))
                    i.then_inc(y_done, 1)

            pe.wait_ge(routed, 1)
            turn_x(0)
            hidden(0)
            turn_x(1)
            hidden(1)
            for u in range(NE):
                turn_a(u)
                if u + 2 < NE:
                    turn_x(u + 2)
                output(u)
                if u + 2 < NE:
                    hidden(u + 2)
            pe.wait_ge(moe_done, 1)
            n_over = pe.value_load(eidi[0:1, NOV:NOV + 1], min_val=0, max_val=NOV)
            with pe.If(n_over > 0):
                with pe.Fori(0, NOV) as i:
                    with pe.If(n_over > i):
                        pe.wait_ge(ov["gx"], (i + 1) * 16)
                        for k in range(KD):
                            m = nc.tensor.transpose(ps[:, 0, k * P:(k + 1) * P], gx[:, 0, k * P:(k + 1) * P], ident[:, :])
                        m.then_inc(ov["xT"], 1)
                        pe.wait_ge(ov["w"], (i + 1) * 32)
                        pe.wait_ge(ov["xg"], i + 1)
                        for k in range(KD):
                            m = mm(ms[:, 0, :], xgT[:, 0, k, :], e13[0][:, k, :], start=(k == 0), stop=(k == KD - 1))
                        m.then_inc(ov["hid"], 1)
                        pe.wait_ge(ov["act"], i + 1)
                        for k in range(DC):
                            m = nc.tensor.transpose(ps[:, 1, k * P:(k + 1) * P], act_sb[:, 0, k * P:(k + 1) * P], ident[:, :])
                        m.then_inc(ov["aT"], 1)
                        pe.wait_ge(ov["at"], i + 1)
                        for half in range(2):
                            for k in range(DC):
                                m = mm(ps[:, 2, half * 512:(half + 1) * 512], aT[:, 0, k, :], e2[0][:, k, half * 512:(half + 1) * 512],
                                       start=(k == 0), stop=(k == DC - 1))
                        m.then_inc(ov["y"], 1)
                        pe.wait_ge(ov["out"], (i + 1) * 16)
                        pe.sem_inc(ov_turns, 1)
                    pe.nop()
            for n, t in enumerate(PE_SUMS):
                pe.wait_ge(yg_in[t], 32)
                for half in range(2):
                    cols = slice(half * 512, (half + 1) * 512)
                    for j in range(2):
                        m = mm(ps[:, n, cols], ident[:, :], yg[:, 2 * t + j, cols], start=(j == 0), stop=(j == 1))
                m.then_inc(pair_sum, 1)

        @block.vector
        def _(dve):
            V = nc.vector
            tt_, ts_, stt = V.tensor_tensor, V.tensor_scalar, V.scalar_tensor_tensor
            n_chain = [0]

            def chain(ins):
                n_chain[0] += 1
                ins.then_inc(dve_chain, 1)

            def settle():
                dve.wait_ge(dve_chain, n_chain[0])

            def link(ins):
                chain(ins)
                settle()

            def ready(name):
                dve.wait_ge(product_ready, place[name] + 1)
                return product(name)

            dve.wait_ge(smt_ready, 1)
            chain(V.tensor_copy(adab[:, :], ms[:, 0, P:P + 6 * KD]))
            V.tensor_copy(smT[:, :], ms[:, 0, 0:NSM]).then_inc(smt_out, 1)
            dve.wait_ge(roots, 1)
            link(V.reciprocal(st[:, 0, :], st[:, 2, :]))
            for t in range(NT):
                i = ts_(xhat[:, t, :], xres[:, t, :], st[:, 0, t:t + 1], None, ALU.mult)
            i.then_inc(xhat_ready, 1)
            dve.wait_ge(smt_out, 1)
            dve.wait_ge(lam_exp, 1)
            link(ts_(lam[:, 2, :], lam[:, 1, :], 2.0, None, ALU.add))
            link(V.reciprocal(lam[:, 3, :], lam[:, 2, :]))
            link(tt_(lam[:, 2, :], lam[:, 1, :], lam[:, 3, :], ALU.mult))
            link(tt_(lam[:, 3, :], lam[:, 2, :], lam[:, 2, :], ALU.mult))
            link(ts_(lam[:, 4, :], lam[:, 3, :], 1 / 17, 1 / 15, ALU.mult, ALU.add))
            for n in (13, 11, 9, 7, 5, 3, 1):
                link(tt_(lam[:, 4, :], lam[:, 4, :], lam[:, 3, :], ALU.mult))
                link(ts_(lam[:, 4, :], lam[:, 4, :], 1 / n, None, ALU.add))
            link(tt_(lam[:, 4, :], lam[:, 4, :], lam[:, 2, :], ALU.mult))
            link(ts_(lam[:, 5, :], smT[:, LAM:LAM + 8], 0.0, None, ALU.min))
            link(stt(lam[:, 5, :], lam[:, 4, :], -2.0, lam[:, 5, :], ALU.mult, ALU.add))
            chain(ts_(lam[:, 3, :], lam[:, 5, :], RGLRU_C / 2, None, ALU.mult))
            ts_(lam[:, 4, :], lam[:, 5, :], -RGLRU_C / 4, None, ALU.mult).then_inc(lam_ready, 1)
            def take_mod(j):
                src = ready(f"aT{j}")[:, 0:512].rearrange("p (m r s) -> p m s r", m=4, r=4)[:, :, 0:2, :]
                V.tensor_reduce(mod[:, 4 * j:4 * j + 4, :], src, AX.X, ALU.add).then_inc(took["D"], 1)

            def add_bias(a, b):
                wait_taken(dve, f"aT{b // 4 - 1}")
                for s in range(2):
                    chain(tt_(mod[:, a:b, s], mod[:, a:b, s], adab[:, a:b], ALU.add))
                settle()

            for j in range(4):
                take_mod(j)
            add_bias(0, 2 * KD)
            for s in range(2):
                i = stt(A1[:, :, s], mod[:, KD:2 * KD, s], 1.0, smT[:, N1:N1 + KD], ALU.add, ALU.mult)
            i.then_inc(mod_out, 1)
            dve.wait_ge(mod_out, 1)
            for k in range(1, KD, 2):
                src = ready(f"xT{k}")
                ts_(hT[:, k, 0:NS], src[:, 0:NS], A1[:, k, 0:1], mod[:, k, 0:1], ALU.mult, ALU.add)
                ts_(hT[:, k, NS:N], src[:, NS:N], A1[:, k, 1:2], mod[:, k, 1:2], ALU.mult, ALU.add).then_inc(took["D"], 1)
            M = XLP - 3
            for ch in range(LC):
                wait_taken(dve, f"xl{ch}")
                settle()
                if ch:
                    dve.wait_ge(conv_ready, ch)

                def cw(j):
                    return smT[:, CW + 4 * j + ch:CW + 4 * j + ch + 1]
                link(ts_(cacc[:, 0:M], xlp[:, ch, 0:M], cw(0), smT[:, CB + ch:CB + ch + 1], ALU.mult, ALU.add))
                link(stt(cacc[:, 0:M], xlp[:, ch, 1:M + 1], cw(1), cacc[:, 0:M], ALU.mult, ALU.add))
                link(stt(cacc[:, 0:M], xlp[:, ch, 2:M + 2], cw(2), cacc[:, 0:M], ALU.mult, ALU.add))
                grid = (lambda ap, j: ap[:, j:j + PADS].rearrange("p (r w) -> p r w", w=PAD)[:, :, 0:GRID_W])
                chain(stt(xc[:, ch, 0:NS].rearrange("p (r w) -> p r w", w=GRID_W), grid(xlp[:, ch, :], 3), cw(3), grid(cacc, 0),
                          ALU.mult, ALU.add))
                stt(xc[:, ch, NS:N], xlp[:, ch, PADS + 3:XLP], cw(3), cacc[:, PADS:M], ALU.mult, ALU.add).then_inc(conv_ready, 1)
            dve.wait_ge(conv_ready, LC)
            take_mod(4)
            take_mod(5)
            for h in range(2):
                if h:
                    take_mod(8)
                    take_mod(9)
                for ch in (2 * h, 2 * h + 1):
                    for s in range(2):
                        j = (ch % 2) * 2 + s
                        wait_taken(dve, f"lr{ch}{s}1")
                        chain(stt(ix[:, j, :], ix[:, j, :], 1.0, xc[:, ch, :], ALU.add, ALU.mult))
                if h == 0:
                    take_mod(6)
                    take_mod(7)
                for ch in (2 * h, 2 * h + 1):
                    for s in range(2):
                        j = (ch % 2) * 2 + s
                        dve.wait_ge(lru_sqrt, 4 * h + j + 1)
                        link(stt(tau[:, j, :], av[:, j, :], 1.0, tau[:, j, :], ALU.add, ALU.mult))
                        link(tt_(ix[:, j, :], ix[:, j, :], tau[:, j, :], ALU.mult))
                        rev = slice(None, None, -1) if s else slice(None)
                        hcol = smT[:, H0 + 4 * s + ch:H0 + 4 * s + ch + 1]
                        for part, init in ((slice(0, NS), hcol), (slice(NS, N), 0.0)):
                            xs = ix[:, j, part][:, rev]
                            chain(V.tensor_tensor_scan(tau[:, j, part][:, rev], av[:, j, part][:, rev], xs, init, ALU.mult, ALU.add))
                        settle()
                        end = N - 1 if s == 0 else NS
                        V.tensor_copy(lfin[:, 4 * s + ch:4 * s + ch + 1], tau[:, j, end:end + 1]).then_inc(lfin_ready, 1)
                    j = (ch % 2) * 2
                    link(tt_(tau[:, j, :], tau[:, j, :], tau[:, j + 1, :], ALU.add))
                    wait_taken(dve, f"yl{ch}")
                    i = tt_(mixT[:, ch, :], mixT[:, ch, :], tau[:, j, :], ALU.mult)
                    if ch % 2 == 0:
                        chain(i)
                i.then_inc(lru_done, 1)
            dve.wait_ge(lru_done, 2)
            take_mod(10)
            take_mod(11)
            for g in range(4):
                dve.wait_ge(zlog, g + 1)
                link(stt(bcum[:, g, :], bcum[:, g, :], 0.0, gt[:, g, :], ALU.min, ALU.subtract))
                if g == 0:
                    dve.wait_ge(scan_mask, 1)
                rev = slice(None, None, -1) if g % 2 else slice(None)
                V.tensor_tensor_scan(bcum[:, g, :][:, rev], gd[:, :], bcum[:, g, :][:, rev], 0.0, ALU.mult, ALU.add).then_inc(bready, 1)

            def modulation():
                add_bias(2 * KD, 6 * KD)
                for s in range(2):
                    chain(V.tensor_copy(A2[:, 4 * s + 0, :], mod[:, 2 * KD:3 * KD, s]))
                    chain(stt(A2[:, 4 * s + 1, :], mod[:, 4 * KD:5 * KD, s], 1.0, smT[:, N2:N2 + KD], ALU.add, ALU.mult))
                    chain(V.tensor_copy(A2[:, 4 * s + 2, :], mod[:, 3 * KD:4 * KD, s]))
                    i = V.tensor_copy(A2[:, 4 * s + 3, :], mod[:, 5 * KD:6 * KD, s])
                    if s == 0:
                        chain(i)
                i.then_inc(mod_out, 1)

            def chunks(ap):
                return ap.rearrange("p (c i) -> p c i", i=CHUNK)

            def differences(g):
                r = 3 * (g % 2)
                s = g % 2
                mid, last = (CHUNK // 2 - 1, CHUNK - 1) if s == 0 else (CHUNK // 2, 0)
                b = chunks(bcum[:, g, :])
                dve.wait_ge(bready, 4)
                if g >= 2:
                    wait_taken(dve, f"at{g - 2}1")
                    wait_taken(dve, f"kT{g - 2}")
                chain(tt_(chunks(gt[:, r, :]), b, b[:, :, mid:mid + 1].to_broadcast([P, NC, CHUNK]), ALU.subtract))
                tt_(chunks(gt[:, r + 2, :]), b[:, :, last:last + 1].to_broadcast([P, NC, CHUNK]), b, ALU.subtract).then_inc(diffs, 1)

            def scale_qk(g):
                r = 3 * (g % 2)
                dve.wait_ge(exps, g + 1)
                tt_(gt[:, r, :], gt[:, r, :], q[:, g // 2, :], ALU.mult)
                tt_(gt[:, r + 1, :], gt[:, r + 1, :], kk[:, g // 2, :], ALU.mult).then_inc(qk_ready, 1)

            def scores(g):
                s = g % 2
                m = mask[:, s:s + 1, :].bitcast(U32).to_broadcast([P, NT, P])
                for hh in range(2):
                    h = 2 * (g // 2) + hh
                    src = ready(f"at{g}{hh}")[:, 0:N].rearrange("p (t i) -> p t i", i=P)
                    dst = att[:, h, :] if s == 0 else attb[:, :]
                    if s and h:
                        dve.wait_ge(att_ready, h)
                    V.copy_predicated(dst.rearrange("p (t i) -> p t i", i=P), m, src).then_inc(took["D"], 1)
                    if s:
                        wait_taken(dve, f"at{g}{hh}")
                        tt_(att[:, h, :], att[:, h, :], attb[:, :], ALU.add).then_inc(att_ready, 1)

            def carry(g):
                s = g % 2
                src = ready(f"kvA{g}")

                def kv(cn, base, first):
                    col = (cn % 2) * 512 + (cn - first) // 2 * DV
                    return base[:, col:col + DV]
                seq = list(range(SC)) if s == 0 else list(range(SC - 1, -1, -1))
                state = sg0[:, g, :]
                dve.wait_ge(qin_ready, g + 1)
                for a, b in zip(seq[:-1], seq[1:]):
                    i = stt(S[:, g, b, :], state, dec[:, g, a:a + 1], kv(a, src, 0), ALU.mult, ALU.add)
                    if b != seq[-1]:
                        link(i)
                    state = S[:, g, b, :]
                i.then_inc(took["D"], 1)
                src = ready(f"kvB{g}")
                a, b = (SC, SC + 1) if s == 0 else (SC + 1, SC)
                link(V.tensor_copy(S[:, g, b, :], kv(a, src, SC)))
                stt(sfin[:, g, :], S[:, g, b, :], dec[:, g, b:b + 1], kv(b, src, SC), ALU.mult, ALU.add).then_inc(took["D"], 1)

            differences(0)
            differences(1)
            modulation()
            dve.wait_ge(att_zero, 1)
            dve.wait_ge(consts, 3)
            dve.wait_ge(sg_in, 16 * 4)
            scale_qk(0)
            for g in range(4):
                scores(g)
                if g + 2 < 4:
                    differences(g + 2)
                if g + 1 < 4:
                    scale_qk(g + 1)
                if g == 0:
                    dve.wait_ge(rowsT, 1)
                    dve.wait_ge(lfinT, 1)
                    V.tensor_copy(rows_t[:, :], ms[0:8 * KD, 0, 0:P]).then_inc(rows_t_out, 1)
                    V.tensor_copy(lfin_t[:, :], ms[0:8, 0, P:2 * P]).then_inc(lfin_t_out, 1)
                carry(g)
            def normed_o(t):
                dve.wait_ge(oroot, t + 1)
                link(V.reciprocal(orms[:, 2, t, :], orms[:, 1, t, :]))
                if t >= 2:
                    dve.wait_ge(product_ready, place[f"oT{t - 2}"] + 1)
                r = orms[:, 2, t, :].rearrange("p (t b a) -> p t b a", t=2, a=1).to_broadcast([P, 2, 2, DV])
                src = ready(f"o{t}").rearrange("p (b n) -> p b n", b=2)[:, :, 0:2 * DV].rearrange("p b (t n) -> p t b n", t=2)
                tt_(otok[:, t % 2, :].rearrange("p (t b n) -> p t b n", t=2, b=2), src, r, ALU.mult).then_inc(took["D"], 1)

            def gated_o(t):
                m = mixT[:, LC:, t * P:(t + 1) * P]
                stt(m, ready(f"oT{t}")[:, 0:512].rearrange("p (h n) -> p h n", h=HEADS), smT[:, GN:GN + 1], m,
                    ALU.mult, ALU.mult).then_inc(took["D"], 1)

            for t in range(NT):
                normed_o(t)
                if t:
                    gated_o(t - 1)
            for t in range(NT):
                seq = 0 if t < ST else 1
                dve.wait_ge(rows_in[seq], 16 * 4)
                if t:
                    dve.wait_ge(sums, 1 + t)
                stt(mtmp, ready(f"mx{t}"), 1.0, rows[seq][0], ALU.mult, ALU.mult).then_inc(took["D"], 1)
                wait_taken(dve, f"mx{t}")
                if t == 0:
                    gated_o(NT - 1)
                tt_(xres[:, t, :], xres[:, t, :], mtmp, ALU.add).then_inc(rd_ready, 1)
                dve.wait_ge(roots, 2 + t)
                link(V.reciprocal(rt[:, 2, t:t + 1], rt[:, 1, t:t + 1]))
                if t >= 2:
                    dve.wait_ge(h2_out[t % 2], 16 * (t // 2))
                    wait_taken(dve, f"hh{t - 2}")
                link(stt(h2[:, t % 2, :], xres[:, t, :], rt[:, 2, t:t + 1], rows[seq][1], ALU.mult, ALU.mult))
                tt_(h2[:, t % 2, :], h2[:, t % 2, :], rows[seq][2], ALU.add).then_inc(h2_ready, 1)
            dve.wait_ge(logits_ready, NT)
            lgv = ms[:, 0, 0:NT * (NG + NE)].rearrange("p (t e) -> p t e", t=NT)
            b20 = rbias[:, :].rearrange("p (a e) -> p a e", a=1).to_broadcast([P, NT, NG + NE])
            link(tt_(lg[:, :, :], lgv, b20, ALU.add))

            def bc(ap, n):
                return ap.rearrange("p (t a) -> p t a", a=1).to_broadcast([P, NT, n])

            w4b = w4[:, :].rearrange("p (a e) -> p a e", a=1).to_broadcast([P, NT, NG])

            def first_max(dst, src, mx, scratch):
                link(V.tensor_reduce(mx, src, AX.X, ALU.max))
                link(tt_(scratch, src, bc(mx, NG), ALU.is_equal))
                link(tt_(scratch, scratch, w4b, ALU.mult))
                link(V.tensor_reduce(rt[:, 7, :], scratch, AX.X, ALU.max))
                link(tt_(dst, scratch, bc(rt[:, 7, :], NG), ALU.is_equal))

            first_max(r4[:, 2, :, :], lg[:, :, 0:NG], rt[:, 3, :], r4[:, 1, :, :])
            tt_(r4[:, 0, :, :], lg[:, :, 0:NG], bc(rt[:, 3, :], NG), ALU.subtract).then_inc(gready, 1)
            le = lg[:, :, NG:]

            def by_group(ap):
                return ap.rearrange("p t (g e) -> p t g e", g=NG)

            group = r4[:, 2, :, :].rearrange("p t (g a) -> p t g a", a=1).to_broadcast([P, NT, NG, EG])

            def outer(dst, e4):
                link(tt_(by_group(dst), e4.rearrange("p t (a e) -> p t a e", a=1).to_broadcast([P, NT, NG, EG]), group, ALU.mult))

            link(tt_(by_group(r16[:, 0, :, :]), by_group(le), group, ALU.mult))
            link(V.tensor_reduce(r4[:, 5, :, :], r16[:, 0, :, :].rearrange("p t (g e) -> p t e g", g=NG), AX.X, ALU.add))
            link(V.tensor_reduce(rt[:, 4, :], r4[:, 5, :, :], AX.X, ALU.max))
            tt_(r4[:, 3, :, :], r4[:, 5, :, :], bc(rt[:, 4, :], EG), ALU.subtract).then_inc(eready, 1)
            dve.wait_ge(gexp, 1)
            link(V.tensor_reduce(rt[:, 5, :], r4[:, 1, :, :], AX.X, ALU.add))
            link(V.reciprocal(rt[:, 5, :], rt[:, 5, :]))
            dve.wait_ge(eexp, 1)
            ex = r4[:, 4, :, :]
            first_max(r4[:, 5, :, :], ex, rt[:, 0, :], r4[:, 7, :, :])
            link(stt(ex, r4[:, 5, :, :], -2.0, ex, ALU.mult, ALU.add))
            first_max(r4[:, 6, :, :], ex, rt[:, 1, :], r4[:, 7, :, :])
            link(tt_(rt[:, 2, :], rt[:, 0, :], rt[:, 1, :], ALU.add))
            link(V.reciprocal(rt[:, 2, :], rt[:, 2, :]))
            link(tt_(rt[:, 2, :], rt[:, 2, :], rt[:, 5, :], ALU.mult))
            for i2 in range(2):
                chain(tt_(rt[:, i2, :], rt[:, i2, :], rt[:, 2, :], ALU.mult))
            outer(r16[:, 0, :, :], r4[:, 5, :, :])
            outer(r16[:, 1, :, :], r4[:, 6, :, :])
            tt_(r16[:, 2, :, :], r16[:, 0, :, :], r16[:, 1, :, :], ALU.add).then_inc(choice, 1)
            oh = r16[:, 0:2, :, :]

            def pick(dst, what):
                link(tt_(oh_scr[:, :, :, :], oh, what, ALU.mult))
                link(V.tensor_reduce(dst.rearrange("p (i t) -> p i t", i=2), oh_scr[:, :, :, :], AX.X, ALU.add))

            def across(row):
                return row.rearrange("p (a b e) -> p a b e", a=1, b=1).to_broadcast([P, 2, NT, NE])

            def full_units(dst, src, op, n, scr):
                m = NT - 1
                link(tt_(scr, src.rearrange("p (n a) -> p n a", a=1).to_broadcast([P, n, m]),
                         thresholds[:, :].rearrange("p (a m) -> p a m", a=1).to_broadcast([P, n, m]), op))
                link(V.tensor_reduce(dst, scr, AX.X, ALU.add))

            pick(rt2[:, 1, :], across(numbers[:, 0:NE]))
            dve.wait_ge(ranks, 1)
            totals = ms[:, 1, 256:256 + NT * NE].rearrange("p (t e) -> p e t", t=NT)
            link(V.tensor_reduce(cnt[:, 0, :], totals, AX.X, ALU.add))
            full_units(cnt[:, 1, :], cnt[:, 0, :], ALU.is_gt, NE, th_scr[:, 0:NE, :])
            link(V.tensor_tensor_scan(cnt[:, 2, :], ones[:, 0:NE], cnt[:, 1, :], 0.0, ALU.mult, ALU.add))
            link(stt(cnt[:, 3, :], cnt[:, 2, :], float(NE - 1), cnt[:, 1, :], ALU.add, ALU.subtract))
            rk = ms[:, 1, 128:128 + NT * NE].rearrange("p (a t e) -> p a t e", a=1, t=NT).to_broadcast([P, 2, NT, NE])
            rank, number, base, beyond, pos, unit = (rt2[:, n, :] for n in range(6))
            pick(rank, rk)
            pick(base, across(cnt[:, 3, :]))
            full_units(beyond, rank, ALU.is_ge, 2 * NT, th_scr[:, 0:2 * NT, :])
            link(stt(pos, beyond, -float(P), rank, ALU.mult, ALU.add))
            link(tt_(base, base, beyond, ALU.add))
            link(tt_(base, base, number, ALU.subtract))
            link(stt(base, beyond, 1.0, base, ALU.min, ALU.mult))
            link(tt_(unit, number, base, ALU.add))

            def each(col, n):
                return col.rearrange("p (c a) -> p c a", a=1).to_broadcast([P, 2 * NT, n])

            def rows_of(row, n):
                return row.rearrange("p (a n) -> p a n", a=1).to_broadcast([P, 2 * NT, n])

            link(tt_(sel_a[:, :, :], rows_of(numbers[:, :], P), each(pos, P), ALU.is_equal))
            link(tt_(sel_b[:, :, NU:2 * NU], rows_of(numbers[:, 0:NU], NU), each(unit, NU), ALU.is_equal))
            tok = tokid[:, :].rearrange("p (a t b) -> p a t b", a=1, b=1).to_broadcast([P, 2, NT, NU])
            link(tt_(sel_b[:, :, 0:NU].rearrange("p (i t) u -> p i t u", i=2), sel_b[:, :, NU:2 * NU].rearrange("p (i t) u -> p i t u", i=2), tok, ALU.mult))
            gates_of = rt[:, 0:2, :].rearrange("p i t -> p (i t)")
            tt_(sel_b[:, :, NU:2 * NU], sel_b[:, :, NU:2 * NU], each(gates_of, NU), ALU.mult).then_inc(onehots, 1)
            link(stt(rank, unit, float(P), pos, ALU.mult, ALU.add))
            chain(V.tensor_copy(yidx[:, :], rank))
            link(tt_(eid_c[:, :, :], cnt[:, 2, :].rearrange("p (a e) -> p a e", a=1).to_broadcast([P, NOV, NE]),
                     numbers[:, 0:NOV].rearrange("p (n a) -> p n a", a=1).to_broadcast([P, NOV, NE]), ALU.is_le))
            link(V.tensor_reduce(eidf[:, 0:NOV], eid_c[:, :, :], AX.X, ALU.add))
            link(ts_(eidf[:, 0:NOV], eidf[:, 0:NOV], float(NE - 1), None, ALU.min))
            link(V.tensor_copy(eidf[:, NOV:NOV + 1], cnt[:, 2, NE - 1:NE]))
            chain(V.tensor_copy(eidi[:, :], eidf[:, :]))
            dve.wait_ge(tables, 1)
            chain(ts_(slot_tok[:, :], ms[:, 0, 128:128 + NU], float(N), None, ALU.add))
            settle()
            V.tensor_copy(slot_gate[:, :], ms[:, 0, 128 + NU:128 + 2 * NU]).then_inc(routed, 1)
            dve.wait_ge(routed, 1)

            def take_x(u):
                dve.wait_ge(x_turned, u + 1)
                if u >= 2:
                    dve.wait_ge(hid, u - 1)
                V.tensor_copy(xgT[:, u % 2, :, :].rearrange("p k n -> p (k n)"), ps[:, 0, :]).then_inc(x_taken, 1)

            def activate(u):
                b = u % 2
                dve.wait_ge(silu, u + 1)
                if u >= 2:
                    dve.wait_ge(a_turned, u - 1)
                stt(act_sb[:, b, :], sact[:, b, :], slot_gate[:, u:u + 1], ms[:, b, DE:2 * DE], ALU.mult, ALU.mult).then_inc(act_ready, 1)

            def take_a(u):
                b = u % 2
                dve.wait_ge(a_turned, u + 1)
                if u >= 2:
                    dve.wait_ge(y_done, 2 * (u - 1))
                V.tensor_copy(aT[:, b, :, :].rearrange("p k n -> p (k n)"), ps[:, 1, 0:DE]).then_inc(a_taken, 1)

            take_x(0)
            take_x(1)
            activate(0)
            activate(1)
            for u in range(NE):
                take_a(u)
                if u + 2 < NE:
                    take_x(u + 2)
                    activate(u + 2)
            dve.wait_ge(moe_done, 1)
            n_over = dve.value_load(eidi[0:1, NOV:NOV + 1], min_val=0, max_val=NOV)
            with dve.If(n_over > 0):
                with dve.Fori(0, NOV) as i:
                    with dve.If(n_over > i):
                        V.tensor_copy(ov_gate[:, :], slot_gate[:, bass.ds(i + NE, 1)])
                        V.tensor_copy(ov_tok[:, :], slot_tok[:, bass.ds(i + NE, 1)]).then_inc(ov["tok"], 1)
                        dve.wait_ge(ov["tok"], i + 1)
                        dve.wait_ge(ov["xT"], i + 1)
                        V.tensor_copy(xgT[:, 0, :, :].rearrange("p k n -> p (k n)"), ps[:, 0, :]).then_inc(ov["xg"], 1)
                        dve.wait_ge(ov["silu"], i + 1)
                        stt(act_sb[:, 0, :], sact[:, 0, :], ov_gate[:, :], ms[:, 0, DE:2 * DE], ALU.mult, ALU.mult).then_inc(ov["act"], 1)
                        dve.wait_ge(ov["aT"], i + 1)
                        V.tensor_copy(aT[:, 0, :, :].rearrange("p k n -> p (k n)"), ps[:, 1, 0:DE]).then_inc(ov["at"], 1)
                        dve.wait_ge(ov["out"], (i + 1) * 16)
                        dve.sem_inc(ov_turns, 1)
                    dve.nop()
            dve.wait_ge(fg_in, 16)
            def add_experts(t):
                seq = 0 if t < ST else 1
                y1, y2 = yg[:, 2 * t, :], yg[:, 2 * t + 1, :]
                if t in PE_SUMS:
                    dve.wait_ge(pair_sum, PE_SUMS.index(t) + 1)
                    link(tt_(y1, ps[:, PE_SUMS.index(t), :], rows[seq][3], ALU.mult))
                else:
                    dve.wait_ge(yg_in[t], 32)
                    link(tt_(y1, y1, y2, ALU.add))
                    link(tt_(y1, y1, rows[seq][3], ALU.mult))
                tt_(xres[:, t, :], xres[:, t, :], y1, ALU.add).then_inc(rd_ready, 1)

            def last_norm(t):
                dve.wait_ge(roots, 2 + NT + t)
                link(V.reciprocal(st[:, 3, t:t + 1], st[:, 2, t:t + 1]))
                stt(xres[:, t, :], xres[:, t, :], st[:, 3, t:t + 1], fing, ALU.mult, ALU.mult).then_inc(ready_out, 1)

            for t in range(NT):
                add_experts(t)
                if t:
                    last_norm(t - 1)
            last_norm(NT - 1)


_INS = ['x_prompt', 'x_sample', 'state_lru', 'state_gla', 'c', 'c_ctx', 'ada_w', 'ada_b', 'norm1_g', 'w_in',
        'conv_w', 'conv_b', 'lru_wr', 'lru_br', 'lru_wi', 'lru_bi', 'lru_lam', 'gla_wg', 'gla_bg',
        'gla_norm_g', 'w_out', 'norm2_g', 'router_gw', 'router_gb', 'router_ew', 'router_eb', 'exp_w13',
        'exp_w2', 'final_g']
_OUTS = ['x_prompt', 'x_sample', 'state_lru', 'state_gla']


def kernel(**inputs):
    import numpy as _np
    import concourse.bacc as _bacc
    from concourse import mybir as _mybir
    from concourse.bass_utils import run_bass_kernel_spmd as _run

    nc = _bacc.Bacc("TRN2", target_bir_lowering=False, num_devices=1)
    arrays, args = {}, []
    for name in _INS:
        a = _np.ascontiguousarray(inputs[name])
        arrays[f"in_{name}_dram"] = a
        args.append(nc.dram_tensor(f"in_{name}_dram", a.shape, _mybir.dt.from_np(a.dtype), kind="ExternalInput").ap())
    for i, like in enumerate(_OUTS):
        a = inputs[like]
        args.append(nc.dram_tensor(f"out_{i}_dram", a.shape, _mybir.dt.from_np(_np.dtype(a.dtype)), kind="ExternalOutput").ap())
    hybrid_step(nc, *args)
    r = _run(nc, [arrays], core_ids=[0])
    return tuple(r.results[0][f"out_{i}_dram"] for i in range(len(_OUTS)))
```
